# Optimizing a Trainium2 kernel written in Bass

```python
import jax, jax.numpy as jnp
from jax import lax
import numpy as np

D_MODEL = 1024
BATCH = 1
SEQ = 1024
DEPTH = 1
DEC_BATCH = 8
DEC_SEQ = 4
PAST_LEN = 1024
PAGE_SIZE = 128

HEAD_DIM = 64
NSA_HEADS = 8
NSA_GROUPS = 2
NSA_HPG = NSA_HEADS // NSA_GROUPS
RET_HEADS = 4
RET_DK = 64
RET_DV = 64
MEM_HEADS = 4
N_MEM = 256
CMP_BLK = 32
CMP_STRIDE = 16
CMP_HID = 256
SLC_BLK = 64
N_SEL = 16
WINDOW = 512
Q_BLK = 128
RET_CHUNK = 128
N_EXPERTS = 32
TOP_K = 4
D_FF = 1024
SWIGLU_LIMIT = 7.0
SWIGLU_ALPHA = 1.702
MOE_BLK = 128
EPS = 1e-6
NEG = -1e30
BIG = 1e9
ROPE_BASE = 10000.0
SLC_RATIO = SLC_BLK // CMP_STRIDE
CMP_OVL = CMP_BLK // CMP_STRIDE - 1

NSA_Q_COLS = NSA_HEADS * HEAD_DIM
NSA_KV_COLS = 2 * NSA_GROUPS * HEAD_DIM
NSA_GATE_COLS = 3 * NSA_HEADS
RET_QK_COLS = RET_HEADS * RET_DK
RET_V_COLS = RET_HEADS * RET_DV
MEM_Q_COLS = MEM_HEADS * HEAD_DIM
SPLIT_SIZES = (NSA_Q_COLS, NSA_KV_COLS, NSA_KV_COLS, NSA_KV_COLS, NSA_GATE_COLS,
               RET_QK_COLS, RET_QK_COLS, RET_V_COLS, RET_V_COLS, MEM_Q_COLS)
IN_COLS = NSA_Q_COLS + 3 * NSA_KV_COLS + NSA_GATE_COLS + 2 * RET_QK_COLS + 2 * RET_V_COLS + MEM_Q_COLS
MIX_WIDTH = NSA_Q_COLS + RET_V_COLS + MEM_Q_COLS

kernel_name = "hymba_nsa_retention_moe_step"

def _rms(x, g):
    xf = x.astype(jnp.float32)
    y = xf * lax.rsqrt(jnp.mean(xf * xf, axis=-1, keepdims=True) + EPS)
    return (y * g.astype(jnp.float32)).astype(x.dtype)

def _norm_k(kv, g):
    return jnp.stack([_rms(kv[:, :, 0], g), kv[:, :, 1]], axis=2)

def _rotary(x, pos):
    half = x.shape[-1] // 2
    inv = ROPE_BASE ** (-jnp.arange(half, dtype=jnp.float32) / half)
    ang = pos.astype(jnp.float32)[:, None] * inv[None, :]
    cos = jnp.cos(ang)[:, None, :]
    sin = jnp.sin(ang)[:, None, :]
    xf = x.astype(jnp.float32)
    x1, x2 = xf[..., :half], xf[..., half:]
    return jnp.concatenate([x1 * cos - x2 * sin, x1 * sin + x2 * cos], axis=-1)

def _project(x, pos, norm1_g, w_in, q_norm_g, k_norm_slc_g, k_norm_win_g, mem_q_norm_g):
    B, S, _ = x.shape
    z = _rms(x, norm1_g) @ w_in
    parts = []
    off = 0
    for n in SPLIT_SIZES:
        parts.append(z[..., off:off + n])
        off += n
    q, kvc, kvs, kvw, gt, rq, rk, rv, rg, mq = parts
    q = _rms(q.reshape(B, S, NSA_GROUPS, NSA_HPG, HEAD_DIM), q_norm_g)
    kvc = kvc.reshape(B, S, 2, NSA_GROUPS, HEAD_DIM)
    kvs = _norm_k(kvs.reshape(B, S, 2, NSA_GROUPS, HEAD_DIM), k_norm_slc_g)
    kvw = _norm_k(kvw.reshape(B, S, 2, NSA_GROUPS, HEAD_DIM), k_norm_win_g)
    gates = jax.nn.sigmoid(gt.astype(jnp.float32)).reshape(B, S, NSA_GROUPS, NSA_HPG, 3)
    rq = _rotary(rq.reshape(B, S, RET_HEADS, RET_DK), pos)
    rk = _rotary(rk.reshape(B, S, RET_HEADS, RET_DK), pos) * (RET_DK ** -0.5)
    rv = rv.reshape(B, S, RET_HEADS, RET_DV)
    mq = _rms(mq.reshape(B, S, MEM_HEADS, HEAD_DIM), mem_q_norm_g)
    return q, kvc, kvs, kvw, gates, rq, rk, rv, rg, mq

def _compress(kv_rows, pe_k, w1_k, w2_k, pe_v, w1_v, w2_v, k_norm_g):
    B, T = kv_rows.shape[:2]
    n_cmp = (T - CMP_BLK) // CMP_STRIDE + 1
    idx = jnp.arange(n_cmp)[:, None] * CMP_STRIDE + jnp.arange(CMP_BLK)[None, :]
    blk = kv_rows[:, idx]

    def phi(x, pe, w1, w2):
        x = (x + pe[:, None, :]).transpose(0, 1, 3, 2, 4).reshape(B, n_cmp, NSA_GROUPS, CMP_BLK * HEAD_DIM)
        return jax.nn.gelu(x @ w1) @ w2

    kc = _rms(phi(blk[:, :, :, 0], pe_k, w1_k, w2_k), k_norm_g)
    vc = phi(blk[:, :, :, 1], pe_v, w1_v, w2_v)
    cend = jnp.arange(n_cmp, dtype=jnp.int32) * CMP_STRIDE + (CMP_BLK - 1)
    return kc, vc, cend

def _slc_blocks(kv):
    B, T = kv.shape[:2]
    n_slc = -(-T // SLC_BLK)
    kv = jnp.pad(kv, ((0, 0), (0, n_slc * SLC_BLK - T), (0, 0), (0, 0), (0, 0)))
    blk = kv.reshape(B, n_slc, SLC_BLK, 2, NSA_GROUPS, HEAD_DIM).transpose(0, 4, 1, 2, 3, 5)
    return blk[..., 0, :], blk[..., 1, :]

def _nsa_core(q, qpos, gates, kc, vc, cend, ks_blk, vs_blk, kw, vw, wpos):
    B, Q = q.shape[:2]
    scale = HEAD_DIM ** -0.5
    mc = cend[None, :] <= qpos[:, None]
    sc = jnp.einsum('bqghd,bngd->bghqn', q, kc).astype(jnp.float32) * scale
    pc = jax.nn.softmax(jnp.where(mc, sc, NEG), axis=-1)
    pc = jnp.where(jnp.any(mc, axis=-1)[:, None], pc, 0.0)
    oc = jnp.einsum('bghqn,bngd->bqghd', pc.astype(vc.dtype), vc)
    n_cmp = kc.shape[1]
    n_slc = ks_blk.shape[2]
    imp = jnp.pad(pc.sum(axis=2), ((0, 0), (0, 0), (0, 0), (CMP_OVL, SLC_RATIO * n_slc - n_cmp)))
    ps = sum(imp[..., r:r + SLC_RATIO * n_slc:SLC_RATIO] for r in range(SLC_RATIO + CMP_OVL))
    bidx = jnp.arange(n_slc, dtype=jnp.int32)
    cur = qpos // SLC_BLK
    forced = (bidx[None] == 0) | (bidx[None] == cur[:, None]) | (bidx[None] == cur[:, None] - 1)
    valid = bidx[None] <= cur[:, None]
    ps = jnp.where(forced, BIG, jnp.where(valid, ps, NEG))
    k_sel = min(N_SEL, n_slc)
    _, sel = lax.top_k(ps, k_sel)
    take = jax.vmap(jax.vmap(lambda blocks, i: blocks[i]))
    s_len = k_sel * SLC_BLK
    ksel = take(ks_blk, sel).reshape(B, NSA_GROUPS, Q, s_len, HEAD_DIM)
    vsel = take(vs_blk, sel).reshape(B, NSA_GROUPS, Q, s_len, HEAD_DIM)
    spos = (sel[..., None] * SLC_BLK + jnp.arange(SLC_BLK, dtype=jnp.int32)).reshape(B, NSA_GROUPS, Q, s_len)
    ms = spos[:, :, None] <= qpos[None, None, None, :, None]
    ss = jnp.einsum('bqghd,bgqsd->bghqs', q, ksel).astype(jnp.float32) * scale
    psel = jax.nn.softmax(jnp.where(ms, ss, NEG), axis=-1)
    osel = jnp.einsum('bghqs,bgqsd->bqghd', psel.astype(vsel.dtype), vsel)
    dpos = qpos[:, None] - wpos[None, :]
    mw = (dpos >= 0) & (dpos < WINDOW) & (wpos[None, :] >= 0)
    sw = jnp.einsum('bqghd,bsgd->bghqs', q, kw).astype(jnp.float32) * scale
    pw = jax.nn.softmax(jnp.where(mw, sw, NEG), axis=-1)
    ow = jnp.einsum('bghqs,bsgd->bqghd', pw.astype(vw.dtype), vw)
    o = (gates[..., 0:1] * oc.astype(jnp.float32) + gates[..., 1:2] * osel.astype(jnp.float32)
         + gates[..., 2:3] * ow.astype(jnp.float32))
    return o.astype(q.dtype)

def _nsa_prompt(q, gates, kvc, kvs, kvw, cmp_w):
    B, S = q.shape[:2]
    kc, vc, cend = _compress(kvc, *cmp_w)
    ks_blk, vs_blk = _slc_blocks(kvs)
    kw_pad = jnp.pad(kvw, ((0, 0), (WINDOW, 0), (0, 0), (0, 0), (0, 0)))
    n_qb = S // Q_BLK
    qb = q.reshape(B, n_qb, Q_BLK, NSA_GROUPS, NSA_HPG, HEAD_DIM).swapaxes(0, 1)
    gb = gates.reshape(B, n_qb, Q_BLK, NSA_GROUPS, NSA_HPG, 3).swapaxes(0, 1)
    starts = jnp.arange(n_qb, dtype=jnp.int32) * Q_BLK

    def body(args):
        qi, gi, s0 = args
        qpos = s0 + jnp.arange(Q_BLK, dtype=jnp.int32)
        kwi = lax.dynamic_slice_in_dim(kw_pad, s0, WINDOW + Q_BLK, axis=1)
        wpos = s0 - WINDOW + jnp.arange(WINDOW + Q_BLK, dtype=jnp.int32)
        return _nsa_core(qi, qpos, gi, kc, vc, cend, ks_blk, vs_blk, kwi[:, :, 0], kwi[:, :, 1], wpos)

    o = lax.map(body, (qb, gb, starts))
    return o.swapaxes(0, 1).reshape(B, S, NSA_Q_COLS)

def _nsa_sample(q, gates, kvc_new, kvs_new, kvw_new, pool_cmp, pool_slc, win_buf, page_table, cmp_w):
    DB, QS = q.shape[:2]

    def gather_pages(pool):
        pages = pool[page_table]
        return pages.reshape(DB, -1, 2, NSA_GROUPS, HEAD_DIM)

    full_c = jnp.concatenate([gather_pages(pool_cmp), kvc_new], axis=1)
    full_s = jnp.concatenate([gather_pages(pool_slc), kvs_new], axis=1)
    past = full_c.shape[1] - QS
    kc, vc, cend = _compress(full_c, *cmp_w)
    ks_blk, vs_blk = _slc_blocks(full_s)
    wb = win_buf.shape[1]
    win = jnp.concatenate([win_buf, kvw_new], axis=1)
    wpos = past - wb + jnp.arange(wb + QS, dtype=jnp.int32)
    qpos = past + jnp.arange(QS, dtype=jnp.int32)
    o = _nsa_core(q, qpos, gates, kc, vc, cend, ks_blk, vs_blk, win[:, :, 0], win[:, :, 1], wpos)
    return o.reshape(DB, QS, NSA_Q_COLS), win[:, QS:]

def _log_decay():
    return jnp.log(1.0 - 2.0 ** (-5.0 - jnp.arange(RET_HEADS, dtype=jnp.float32)))

def _ret_chunk(R, q, k, v):
    C = q.shape[1]
    lg = _log_decay()
    idx = jnp.arange(C, dtype=jnp.float32)
    diff = idx[:, None] - idx[None, :]
    dmask = jnp.where(diff >= 0, jnp.exp(jnp.maximum(diff, 0.0)[None] * lg[:, None, None]), 0.0)
    s = jnp.einsum('bnhd,bmhd->bhnm', q, k) * dmask
    o = jnp.einsum('bhnm,bmhe->bnhe', s, v)
    xi = jnp.exp((idx + 1.0)[:, None] * lg[None, :])
    o = o + jnp.einsum('bnhd,bhde->bnhe', q, R) * xi[None, :, :, None]
    zeta = jnp.exp((C - 1.0 - idx)[:, None] * lg[None, :])
    R = jnp.exp(C * lg)[None, :, None, None] * R + jnp.einsum('bmhd,bmhe->bhde', k * zeta[None, :, :, None], v)
    return o, R

def _retention_prompt(rq, rk, rv):
    B, S = rq.shape[:2]
    n = S // RET_CHUNK

    def to_chunks(a):
        return a.reshape(B, n, RET_CHUNK, *a.shape[2:]).swapaxes(0, 1)

    R0 = jnp.zeros((B, RET_HEADS, RET_DK, RET_DV), jnp.float32)

    def step(R, xs):
        o, R = _ret_chunk(R, *xs)
        return R, o

    R, o = lax.scan(step, R0, (to_chunks(rq), to_chunks(rk), to_chunks(rv.astype(jnp.float32))))
    return o.swapaxes(0, 1).reshape(B, S, RET_HEADS, RET_DV), R

def _ret_out(o, rg, g):
    B, S = o.shape[:2]
    gate = jax.nn.silu(rg.astype(jnp.float32)).reshape(B, S, RET_HEADS, RET_DV)
    return (_rms(o, g) * gate).reshape(B, S, RET_V_COLS)

def _mem_kv(mem, mem_norm_g, w_mem_kv, mem_k_norm_g):
    B = mem.shape[0]
    kv = (_rms(mem, mem_norm_g) @ w_mem_kv).reshape(B, N_MEM, 2, MEM_HEADS, HEAD_DIM)
    return _norm_k(kv, mem_k_norm_g)

def _mem_attend(mq, mkv):
    B, S = mq.shape[:2]
    s = jnp.einsum('bqhd,bmhd->bhqm', mq, mkv[:, :, 0]).astype(jnp.float32) * (HEAD_DIM ** -0.5)
    p = jax.nn.softmax(s, axis=-1)
    o = jnp.einsum('bhqm,bmhd->bqhd', p.astype(mkv.dtype), mkv[:, :, 1])
    return o.reshape(B, S, MEM_Q_COLS)

def _moe(h, w_router, b_router, w_up, b_up, w_down, b_down):
    T = h.shape[0]
    A = T * TOP_K
    logits = (h @ w_router).astype(jnp.float32) + b_router.astype(jnp.float32)
    top_val, top_idx = lax.top_k(logits, TOP_K)
    gate = jax.nn.softmax(top_val, axis=-1).reshape(-1)
    e_flat = top_idx.reshape(-1)
    order = jnp.argsort(e_flat)
    e_sorted = e_flat[order]
    counts = jnp.bincount(e_flat, length=N_EXPERTS)
    padded = (counts + MOE_BLK - 1) // MOE_BLK * MOE_BLK
    pad_end = jnp.cumsum(padded)
    pad_start = pad_end - padded
    start = jnp.cumsum(counts) - counts
    dest = pad_start[e_sorted] + jnp.arange(A) - start[e_sorted]
    n_blk = (A + N_EXPERTS * (MOE_BLK - 1) + MOE_BLK - 1) // MOE_BLK
    P = n_blk * MOE_BLK
    slot_tok = jnp.full((P,), T, jnp.int32).at[dest].set((order // TOP_K).astype(jnp.int32))
    slot_gate = jnp.zeros((P,), jnp.float32).at[dest].set(gate[order])
    blk_expert = jnp.minimum(jnp.searchsorted(pad_end, jnp.arange(n_blk) * MOE_BLK, side='right'), N_EXPERTS - 1)
    h_pad = jnp.concatenate([h, jnp.zeros((1, h.shape[1]), h.dtype)], axis=0)
    xb = h_pad[slot_tok].reshape(n_blk, MOE_BLK, h.shape[1])

    def expert_block(args):
        xblk, e = args
        up = xblk @ w_up[e] + b_up[e]
        x_glu = jnp.minimum(up[..., :D_FF], SWIGLU_LIMIT)
        x_lin = jnp.clip(up[..., D_FF:], -SWIGLU_LIMIT, SWIGLU_LIMIT)
        act = x_glu * jax.nn.sigmoid(SWIGLU_ALPHA * x_glu) * (x_lin + 1.0)
        return act @ w_down[e] + b_down[e]

    yb = lax.map(expert_block, (xb, blk_expert)).reshape(P, h.shape[1])
    yb = yb * slot_gate[:, None].astype(yb.dtype)
    return jax.ops.segment_sum(yb, slot_tok, num_segments=T + 1)[:T]

def setup_inputs(seed: int = 0) -> dict:
    key = jax.random.key(seed)
    keys = iter(jax.random.split(key, 48))
    f32 = jnp.float32
    n_pages = PAST_LEN // PAGE_SIZE
    n_phys = (DEC_BATCH * n_pages * 5) // 4
    win_buf = min(WINDOW, PAST_LEN)

    def normal(shape, scale):
        return jax.random.normal(next(keys), shape, f32) * scale

    def gain(shape):
        return 1.0 + normal(shape, 0.02)

    perm = jax.random.permutation(next(keys), n_phys)
    page_table = perm[:DEC_BATCH * n_pages].reshape(DEC_BATCH, n_pages).astype(jnp.int32)
    L = DEPTH
    return {
        'x_prompt': normal((BATCH, SEQ, D_MODEL), 1.0),
        'x_sample': normal((DEC_BATCH, DEC_SEQ, D_MODEL), 1.0),
        'mem_prompt': normal((BATCH, N_MEM, D_MODEL), 1.0),
        'cache_cmp_kv': normal((L, n_phys, PAGE_SIZE, 2, NSA_GROUPS, HEAD_DIM), 1.0),
        'cache_slc_kv': normal((L, n_phys, PAGE_SIZE, 2, NSA_GROUPS, HEAD_DIM), 1.0),
        'cache_win_kv': normal((L, DEC_BATCH, win_buf, 2, NSA_GROUPS, HEAD_DIM), 1.0),
        'state_ret': normal((L, DEC_BATCH, RET_HEADS, RET_DK, RET_DV), 1.0),
        'cache_mem_kv': normal((L, DEC_BATCH, N_MEM, 2, MEM_HEADS, HEAD_DIM), 1.0),
        'page_table': page_table,
        'norm1_g': gain((L, D_MODEL)),
        'w_in': normal((L, D_MODEL, IN_COLS), D_MODEL ** -0.5),
        'q_norm_g': gain((L, HEAD_DIM)),
        'k_norm_cmp_g': gain((L, HEAD_DIM)),
        'k_norm_slc_g': gain((L, HEAD_DIM)),
        'k_norm_win_g': gain((L, HEAD_DIM)),
        'cmp_pe_k': normal((L, CMP_BLK, HEAD_DIM), 0.1),
        'cmp_w1_k': normal((L, CMP_BLK * HEAD_DIM, CMP_HID), (CMP_BLK * HEAD_DIM) ** -0.5),
        'cmp_w2_k': normal((L, CMP_HID, HEAD_DIM), CMP_HID ** -0.5),
        'cmp_pe_v': normal((L, CMP_BLK, HEAD_DIM), 0.1),
        'cmp_w1_v': normal((L, CMP_BLK * HEAD_DIM, CMP_HID), (CMP_BLK * HEAD_DIM) ** -0.5),
        'cmp_w2_v': normal((L, CMP_HID, HEAD_DIM), CMP_HID ** -0.5),
        'ret_norm_g': gain((L, RET_DV)),
        'mem_norm_g': gain((L, D_MODEL)),
        'w_mem_kv': normal((L, D_MODEL, 2 * MEM_HEADS * HEAD_DIM), D_MODEL ** -0.5),
        'mem_q_norm_g': gain((L, HEAD_DIM)),
        'mem_k_norm_g': gain((L, HEAD_DIM)),
        'w_out': normal((L, MIX_WIDTH, D_MODEL), MIX_WIDTH ** -0.5),
        'norm2_g': gain((L, D_MODEL)),
        'w_router': normal((L, D_MODEL, N_EXPERTS), D_MODEL ** -0.5),
        'b_router': normal((L, N_EXPERTS), 0.01),
        'w_up': normal((L, N_EXPERTS, D_MODEL, 2 * D_FF), D_MODEL ** -0.5),
        'b_up': normal((L, N_EXPERTS, 2 * D_FF), 0.01),
        'w_down': normal((L, N_EXPERTS, D_FF, D_MODEL), D_FF ** -0.5),
        'b_down': normal((L, N_EXPERTS, D_MODEL), 0.01),
    }

def reference(x_prompt, x_sample, mem_prompt, cache_cmp_kv, cache_slc_kv, cache_win_kv, state_ret,
              cache_mem_kv, page_table, norm1_g, w_in, q_norm_g, k_norm_cmp_g, k_norm_slc_g, k_norm_win_g,
              cmp_pe_k, cmp_w1_k, cmp_w2_k, cmp_pe_v, cmp_w1_v, cmp_w2_v, ret_norm_g, mem_norm_g, w_mem_kv,
              mem_q_norm_g, mem_k_norm_g, w_out, norm2_g, w_router, b_router, w_up, b_up, w_down, b_down):
    B, S, D = x_prompt.shape
    DB, QS, _ = x_sample.shape
    past = page_table.shape[1] * cache_cmp_kv.shape[2]
    pos_p = jnp.arange(S, dtype=jnp.int32)
    pos_s = past + jnp.arange(QS, dtype=jnp.int32)
    xp, xs = x_prompt, x_sample
    cmp_p, slc_p, win_p, ret_p, mem_p = [], [], [], [], []
    cmp_s, slc_s, win_s, ret_s = [], [], [], []
    for l in range(DEPTH):
        cmp_w = (cmp_pe_k[l], cmp_w1_k[l], cmp_w2_k[l], cmp_pe_v[l], cmp_w1_v[l], cmp_w2_v[l], k_norm_cmp_g[l])
        q, kvc, kvs, kvw, gts, rq, rk, rv, rg, mq = _project(
            xp, pos_p, norm1_g[l], w_in[l], q_norm_g[l], k_norm_slc_g[l], k_norm_win_g[l], mem_q_norm_g[l])
        o_nsa = _nsa_prompt(q, gts, kvc, kvs, kvw, cmp_w)
        o_ret, r_new = _retention_prompt(rq, rk, rv)
        mkv = _mem_kv(mem_prompt, mem_norm_g[l], w_mem_kv[l], mem_k_norm_g[l])
        o_mem = _mem_attend(mq, mkv)
        mix = jnp.concatenate([o_nsa, _ret_out(o_ret, rg, ret_norm_g[l]).astype(xp.dtype),
                               o_mem.astype(xp.dtype)], axis=-1)
        xp = xp + mix @ w_out[l]
        cmp_p.append(kvc)
        slc_p.append(kvs)
        win_p.append(kvw[:, S - min(WINDOW, S):])
        ret_p.append(r_new)
        mem_p.append(mkv)
        q, kvc, kvs, kvw, gts, rq, rk, rv, rg, mq = _project(
            xs, pos_s, norm1_g[l], w_in[l], q_norm_g[l], k_norm_slc_g[l], k_norm_win_g[l], mem_q_norm_g[l])
        o_nsa, win_new = _nsa_sample(q, gts, kvc, kvs, kvw, cache_cmp_kv[l], cache_slc_kv[l],
                                     cache_win_kv[l], page_table, cmp_w)
        o_ret, r_new = _ret_chunk(state_ret[l].astype(jnp.float32), rq, rk, rv.astype(jnp.float32))
        o_mem = _mem_attend(mq, cache_mem_kv[l])
        mix = jnp.concatenate([o_nsa, _ret_out(o_ret, rg, ret_norm_g[l]).astype(xs.dtype),
                               o_mem.astype(xs.dtype)], axis=-1)
        xs = xs + mix @ w_out[l]
        cmp_s.append(kvc)
        slc_s.append(kvs)
        win_s.append(win_new)
        ret_s.append(r_new)
        h_all = jnp.concatenate([_rms(xp, norm2_g[l]).reshape(B * S, D),
                                 _rms(xs, norm2_g[l]).reshape(DB * QS, D)], axis=0)
        y_all = _moe(h_all, w_router[l], b_router[l], w_up[l], b_up[l], w_down[l], b_down[l])
        xp = xp + y_all[:B * S].reshape(B, S, D)
        xs = xs + y_all[B * S:].reshape(DB, QS, D)
    return (xp, xs, jnp.stack(cmp_p), jnp.stack(slc_p), jnp.stack(win_p), jnp.stack(ret_p), jnp.stack(mem_p),
            jnp.stack(cmp_s), jnp.stack(slc_s), jnp.stack(win_s), jnp.stack(ret_s))


_drawn_inputs = setup_inputs


def setup_inputs(seed=0):
    import zlib

    import numpy as np

    out = dict(_drawn_inputs(seed))
    spreads = {}
    factors = {'q_norm_g': 4.623,
     'k_norm_cmp_g': 8.0,
     'k_norm_slc_g': 3.905,
     'k_norm_win_g': 4.114,
     'ret_norm_g': 3.249,
     'mem_norm_g': 2.801,
     'mem_q_norm_g': 8.0,
     'mem_k_norm_g': 4.068,
     'b_up': 8.0,
     'b_down': 8.0}
    for name, (base, spread) in spreads.items():
        noise = np.random.default_rng([zlib.crc32(name.encode()), seed]).standard_normal(out[name].shape)
        drawn = base * np.exp(spread * noise) if base else spread * noise
        out[name] = __import__('jax').numpy.asarray(drawn.astype(out[name].dtype))
    for name, factor in factors.items():
        out[name] = (out[name] * factor).astype(out[name].dtype)
    return out
```

```python
import concourse.bass as bass
from concourse import mybir
from contextlib import ExitStack

ALU = mybir.AluOpType
ACT = mybir.ActivationFunctionType
AX = mybir.AxisListType
F32 = mybir.dt.float32
BF16 = mybir.dt.bfloat16
I32 = mybir.dt.int32

P = 128
D = 1024
KC = D // P
S = 1024
PT = S // P
DB, QS = 8, 4
SR = DB * QS
T = S + SR
NT = PT + 1
HD = 64
G, HPG = 2, 4
NMEM = 256
MT = NMEM // P
IN = 2584
CQ, CKC, CKS, CKW, CGT, CRQ, CRK, CRV, CRG, CMQ = 0, 512, 768, 1024, 1280, 1304, 1560, 1816, 2072, 2328
EPS = 1e-6
NEG = -1e30
NCMP = 63
HID = 256
PAGES, PAGE = 8, 128
POOL_PAGES = (1, 4, 7)
WIN = 512
NE, TOPK, FF = 32, 4, 1024
ALPHA, LIMIT = 1.702, 7.0
CAP = 176
WIDTHS = (128, 136, 144, 152, 160, CAP)
OB = 128
OB_MAX = -(-(T - CAP) // OB)
NOB = max(min((T * TOPK - n * (CAP + 1 - OB)) // OB, n * OB_MAX) for n in range(1, NE + 1))
NSLOT = CAP * NE + NOB * OB

def shape_tables():
    import numpy as np
    f = np.float32
    p = np.arange(P)
    tab = {}
    tab["ident"] = np.eye(P, dtype=f)
    tab["causal"] = np.where(p[None, :] <= p[:, None], 0, NEG).astype(f)
    tab["winlow"] = np.where(p[None, :] > p[:, None], 0, NEG).astype(f)
    cend = np.arange(NCMP) * 16 + 31
    qpos = np.arange(PT)[None, :, None] * P + p[:, None, None]
    tab["cmpmask"] = np.where(cend[None, None, :] <= qpos, 0, NEG).astype(f).reshape(P, -1)
    tab["anycmp"] = (p >= 31).astype(f)[:, None]
    inv = (f(10000.0) ** (-np.arange(32, dtype=f) / f(32))).astype(f)
    pos = np.zeros((P, NT), f)
    for t in range(PT):
        pos[:, t] = t * P + p
    pos[:SR, PT] = S + np.arange(SR) % QS
    ang = (pos[:, :, None] * inv).astype(f).astype(np.float64)
    tab["cos"] = np.cos(ang).astype(f).reshape(P, -1)
    tab["sin"] = np.sin(ang).astype(f).reshape(P, -1)
    lg = np.log(1.0 - 2.0 ** (-5.0 - np.arange(4)))
    dn = p[None, None, :] - p[:, None, None]
    dm = np.where(dn >= 0, np.exp(np.maximum(dn, 0) * lg[None, :, None]), 0) * HD ** -0.5
    tab["dmaskT"] = dm.astype(f).reshape(P, -1)
    xi = np.zeros((P, 2, 4)); ze = np.zeros((P, 2, 4))
    xi[:, 0] = np.exp((p[:, None] + 1.0) * lg)
    ze[:, 0] = np.exp((P - 1.0 - p[:, None]) * lg) * HD ** -0.5
    i = p % QS
    xi[:, 1] = np.exp((i[:, None] + 1.0) * lg)
    ze[:, 1] = np.exp((QS - 1.0 - i[:, None]) * lg) * HD ** -0.5
    tab["xi"] = xi.astype(f).reshape(P, -1)
    tab["zeta"] = ze.astype(f).reshape(P, -1)
    dec = np.zeros((P, 2, 2))
    for pair in range(2):
        h = 2 * pair + (p >= 64)
        dec[:, 0, pair] = np.exp(P * lg[h])
        dec[:, 1, pair] = np.exp(QS * lg[h])
    tab["decay"] = dec.astype(f).reshape(P, -1)
    a = np.arange(SR)
    same = (a[:, None] // QS) == (a[None, :] // QS)
    dn = a[None, :] - a[:, None]
    ds = np.zeros((P, 4, SR))
    ds[:SR] = np.where((same & (dn >= 0))[:, None, :], np.exp(np.maximum(dn, 0)[:, None, :] * lg[None, :, None]), 0) * HD ** -0.5
    tab["dmaskTs"] = ds.astype(f).reshape(P, -1)
    bm = np.zeros((P, DB)); bm[a, a // QS] = 1
    tab["ofrow"] = bm.astype(f)
    rb, rq = p // 32, p % QS
    nm = np.full((P, 2, SR), NEG)
    for half in range(2):
        for j in range(SR):
            ok = (j // QS == half * 4 + rb) & (j % QS <= rq)
            nm[ok, half, j] = 0
    tab["newmask"] = nm.astype(f).reshape(P, -1)
    tab["oldwin"] = np.where(np.arange(WIN)[None, :] > rq[:, None], 0, NEG).astype(f)
    grp = (p // 16) * 4 + rq
    tab["headsum"] = (grp[:, None] == grp[None, :]).astype(f)
    tok, gc = (p // 32) * QS + rq, (p % 32) // QS
    rs = np.zeros((P, 2, P)); rs[tok, 0, p] = 1; rs[16 + tok, 1, p] = 1
    tab["rowsel"] = rs.astype(f).reshape(P, -1)
    tab["rowhead"] = (gc[:, None] == np.arange(8)[None, :]).astype(f)
    tab["blockidx"] = np.tile(np.arange(1, 15, dtype=f), (P, 1))
    tab["blockmean"] = ((p[:, None] // 64) == (p[None, :] // 64)).astype(f) / 64
    tab["before"] = (p[:, None] < p[None, :]).astype(f)
    tab["expert"] = np.tile(np.arange(NE, dtype=f), (P, 1))
    tab["blk"] = np.tile(np.arange(NOB, dtype=f), (P, 1))
    tab["insample"] = (p < SR).astype(f)[:, None]
    at, packed = {}, []
    early = ("ident", "cos", "sin", "dmaskT", "xi", "zeta", "decay")
    for names in (early, [n for n in tab if n not in early]):
        cols, off = [], 0
        for n in names:
            at[n] = (off, tab[n].shape[1])
            off += tab[n].shape[1]
            cols.append(tab[n])
        packed.append(np.ascontiguousarray(np.concatenate(cols, 1)))
    tok = np.full((P, NT), T, np.int32)
    for t in range(NT):
        n = P if t < PT else SR
        tok[:n, t] = t * P + np.arange(n)
    return packed, at, tok


class Ctx:
    pass


def rows(t):
    return SR if t == PT else P


def bc(ap, n):
    return ap.unsqueeze(2).broadcast_to([ap.shape[0], ap.shape[1], n])


def phase_project(nc, k):
    i, o, at, C = k.i, k.o, k.at, k.C
    NA = NT + MT
    SL = [(n * 512, min(512, IN - n * 512)) for n in range(6)]
    slices = lambda t: SL if t < NT else [(0, 512)]
    zs = lambda t: 6 * min(t, NT) + max(t - NT, 0)
    pg = lambda t: 4 * min(t, NT) + max(t - NT, 0)
    with ExitStack() as ctx:
        sb = lambda n, s, d=F32: ctx.enter_context(nc.sbuf_tensor(n, s, d))
        ps = lambda n, s, d=F32: ctx.enter_context(nc.psum_tensor(n, s, d))
        sem = k.sem
        w = sb("w_in", [P, KC, IN])
        wm = w[:, :, 0:512]
        xb = sb("x", [P, D])
        xs = sb("xs", [P, D])
        xnT = [sb(f"xnT{j}", [P, KC, P]) for j in range(2)]
        nrm = sb("nrm", [P, D])
        tr = sb("rotary_t", [P, 2, 512])
        rot, kz = k.rot, k.kz
        z = [sb(f"z{j}", [P, IN]) for j in range(2)]
        qxi = sb("qxi", [P, 256])
        sTm = sb("sTm", [P, 4, P])
        Rst = k.Rst
        xss = sb("xss", [P, 4 * NA])
        hss = sb("hss", [P, 2, 16])
        ghead = k.logits[:].rearrange("p t e -> p (t e)")[:, 0:3 * HD].rearrange("p (j d) -> p j d", d=HD)
        gx = sb("gx", [P, 2, KC])
        gq = sb("gq", [P, 2])
        xT = [ps(f"xTp{j}", [P, 4, P]) for j in range(2)]
        zp = [ps(f"zp{j}", [P, 512]) for j in range(2)]
        pt = [ps(f"pt{j}", [P, 4, P]) for j in range(2)]
        sTp = ps("sTp", [P, 4, P])
        oR = ps("oR", [P, 512])
        s_c = sem("consts_loaded")
        s_w = sem("w_in_loaded")
        s_x = sem("x_loaded")
        s_xss, s_xms, s_xrt, s_xs = sem("x_squares_summed"), sem("x_mean_square"), sem("x_root"), sem("xs_ready")
        s_xT, s_xnT = sem("xT_done"), sem("xnT_ready")
        s_zmm, s_zev = sem("z_done"), sem("z_evicted")
        s_hsq, s_hms, s_hrt, s_nrm, s_rot = sem("head_squares"), sem("head_mean_square"), sem("head_root"), sem("nrm_ready"), sem("rot_ready")
        s_pt, s_ptev = sem("post_transposed"), sem("post_evicted")
        s_sT, s_sTm, s_o, s_R = sem("ret_scores"), sem("ret_scores_masked"), sem("ret_out"), sem("ret_state_updated")
        s_pool = sem("z_parts_copied")
        s_row = sem("even_heads_done")
        s_out = [sem(f"z_stored{j}") for j in range(2)]
        s_dc, s_g0 = sem("project_dve_chain"), sem("gains_ready")
        xsrc = lambda t: (i["x_prompt"][0, t * P:(t + 1) * P, :] if t < PT else
                          i["x_sample"].rearrange("b s d -> (b s) d") if t == PT else
                          i["mem_prompt"][0, (t - NT) * P:(t - NT + 1) * P, :])
        nout = lambda t: (4 if t == PT else 1 if t > PT else 3 if t >= 4 else 2)
        stored = lambda t: 16 * sum(nout(u) for u in range(t % 2, t + 1, 2))
        steps = lambda t, n: [n] if t < NT else [1, 2, 3, 4, 5]
        block = ctx.enter_context(nc.Block())

        @block.sync
        def _(sp):
            def load_x(t):
                if t >= 1:
                    sp.wait_ge(s_xs, t)
                sp.dma_start(xb[:rows(t), :], xsrc(t)).then_inc(s_x, 16)

            load_x(0)
            sp.dma_start(C[:], i["tables_a"]).then_inc(s_c, 16)
            sp.dma_start(k.tok[:], i["tokens"]).then_inc(s_c, 16)
            sp.dma_start(k.pages[:], i["page_table"].rearrange("(o b) p -> o (b p)", o=1)).then_inc(s_c, 16)
            with nc.allow_non_contiguous_dma(reason="gain vectors, small"):
                for j, n in enumerate(("norm1_g", "mem_norm_g")):
                    sp.dma_start(gx[:, j, :], i[n].rearrange("l (c p) -> p (l c)", p=P)).then_inc(s_c, 16)
                for j, n in enumerate(("q_norm_g", "mem_q_norm_g")):
                    for half in range(2):
                        sp.dma_start(gq[64 * half:64 * half + 64, j:j + 1], i[n].rearrange("l d -> d l")).then_inc(s_c, 16)
            for j, n in enumerate(("k_norm_slc_g", "k_norm_win_g", "mem_k_norm_g")):
                sp.dma_start(ghead[:, j, :], i[n].broadcast_to([P, HD])).then_inc(s_c, 16)
            wv = i["w_in"][0].rearrange("(c p) n -> p c n", p=P)
            for n, (c0, cn) in enumerate(SL):
                sp.dma_start(w[:, :, c0:c0 + cn], wv[:, :, c0:c0 + cn]).then_inc(s_w, 16)
                if n == 0:
                    load_x(1)
                sp.wait_ge(s_w, 16 * (n + 1))
            for t in range(NA):
                if t == NT - 1:
                    sp.wait_ge(s_zmm, zs(NT - 1) + 1)
                    sp.dma_start(wm, i["w_mem_kv"][0].rearrange("(c p) n -> p c n", p=P)).then_inc(s_w, 16)
                if t + 2 < NA:
                    load_x(t + 2)
                sp.wait_ge(s_nrm, t + 1)
                zz, R = z[t % 2], rows(t)
                so = s_out[t % 2]
                flat = lambda a: a.rearrange("l b s k g d -> (l b s) (k g d)")
                if t < PT:
                    sp.dma_start(flat(o["cmp_p"])[t * P:(t + 1) * P], zz[:, CKC:CKC + 256]).then_inc(so, 16)
                    sp.dma_start(flat(o["slc_p"])[t * P:(t + 1) * P], zz[:, CKS:CKS + 256]).then_inc(so, 16)
                    if t >= 4:
                        sp.dma_start(flat(o["win_p"])[(t - 4) * P:(t - 3) * P], zz[:, CKW:CKW + 256]).then_inc(so, 16)
                elif t == PT:
                    sp.dma_start(flat(o["cmp_s"]), zz[:R, CKC:CKC + 256]).then_inc(so, 16)
                    sp.dma_start(flat(o["slc_s"]), zz[:R, CKS:CKS + 256]).then_inc(so, 16)
                    ws = o["win_s"].rearrange("l b s k g d -> (l b) s (k g d)")
                    sp.dma_start(ws[:, WIN - QS:, :], zz[:R, CKW:CKW + 256]).then_inc(so, 16)
                    sp.dma_start(ws[:, :WIN - QS, :], i["cache_win_kv"].rearrange("l b s k g d -> (l b) s (k g d)")[:, QS:, :]).then_inc(so, 16)
                else:
                    sp.dma_start(flat(o["mem_p"])[(t - NT) * P:(t - NT + 1) * P], zz[:, 0:512]).then_inc(so, 16)
            for j in range(2):
                last = NA - 1 if (NA - 1) % 2 == j else NA - 2
                sp.wait_ge(s_out[j], stored(last))

        @block.gpsimd
        def _(pool):
            for t in range(NA):
                R, zz = rows(t), z[t % 2]
                pool.wait_ge(s_zev, zs(t + 1))
                if t < NT:
                    nc.gpsimd.tensor_copy(k.vs[:R, t, :], zz[:R, CKS + 128:CKS + 256])
                    nc.gpsimd.tensor_copy(k.vw[:R, t, :], zz[:R, CKW + 128:CKW + 256])
                    nc.gpsimd.tensor_copy(k.rg[:R, t, :], zz[:R, CRG:CRG + 256])
                    if t == PT:
                        nc.gpsimd.tensor_copy(k.rvs[:], zz[:R, CRV:CRV + 256])
                    nc.gpsimd.tensor_copy(k.gate[:R, t, :], zz[:R, CGT:CGT + 24]).then_inc(s_pool, 1)
                else:
                    nc.gpsimd.tensor_copy(k.mv[:, t - NT, :], zz[:, 256:512]).then_inc(s_pool, 1)

        @block.tensor
        def _(pe):
            ident = C[:, at["ident"]]

            def pre(t):
                R = rows(t)
                pe.wait_ge(s_xs, t + 1)
                if t >= 1:
                    pe.wait_ge(s_xnT, 2 * t)
                for c in range(KC):
                    mm = nc.tensor.transpose(xT[c // 4][:, c % 4, :R], xs[:R, c * P:(c + 1) * P], ident[:R, :R])
                mm.then_inc(s_xT, 1)

            def project(t):
                R = rows(t)
                pe.wait_ge(s_xnT, 2 * t + 2)
                for n, (c0, cn) in enumerate(slices(t)):
                    s = zs(t) + n
                    if t == 0:
                        pe.wait_ge(s_w, 16 * (n + 1))
                    if t == NT and n == 0:
                        pe.wait_ge(s_w, 16 * 7)
                    if s >= 2:
                        pe.wait_ge(s_zev, s - 1)
                    ww = w if t < NT else wm
                    for c in range(KC):
                        mm = nc.tensor.matmul(zp[s % 2][:R, :cn], xnT[t % 2][:, c, :R], ww[:, c, c0:c0 + cn],
                                              start=(c == 0), stop=(c == KC - 1))
                    mm.then_inc(s_zmm, 1)
                    for step in steps(t, n):
                        if step == 1 and t + 1 < NA:
                            pre(t + 1)
                        if step >= 2 and t >= 1:
                            post(t - 1, step)

            def turn(t, j, srcs):
                g = pg(t) + j
                R = rows(t)
                if g >= 2:
                    pe.wait_ge(s_ptev, g - 1)
                for m, src in enumerate(srcs):
                    mm = nc.tensor.transpose(pt[g % 2][:, m, :R], src, ident[:R, :R])
                mm.then_inc(s_pt, 1)

            def post(t, step):
                R, zz = rows(t), z[t % 2]
                if step == 2:
                    pe.wait_ge(s_nrm, t + 1)
                    if t >= NT:
                        turn(t, 0, [zz[:, 0:128], zz[:, 128:256]])
                        return
                    turn(t, 0, [nrm[:R, c * P:(c + 1) * P] for c in range(4)])
                    turn(t, 1, [zz[:R, CKS:CKS + 128], zz[:R, CKW:CKW + 128], nrm[:R, 768:896], nrm[:R, 896:1024]])
                if t >= NT:
                    return
                if step == 3:
                    pe.wait_ge(s_rot, t + 1)
                    turn(t, 2, [rot[:R, 0:128], rot[:R, 128:256], qxi[:R, 0:128], qxi[:R, 128:256]])
                    turn(t, 3, [rot[:R, 256:384], rot[:R, 384:512]])
                if t < PT and step == 4:
                    retention_scores(t)
                if t < PT and step == 5:
                    retention_out(t)

            def retention_scores(t):
                pe.wait_ge(s_ptev, pg(t) + 4)
                for h in (0, 2, 1, 3):
                    b = 64 * (h % 2)
                    mm = nc.tensor.matmul(sTp[:, h, :], k.rT[b:b + 64, 4 + h // 2, :], k.rT[b:b + 64, h // 2, :],
                                          start=True, stop=True)
                    if h == 2:
                        mm.then_inc(s_row, 1)
                        pe.wait_ge(s_row, 2 * t + 1)
                mm.then_inc(s_sT, 1)

            def retention_out(t):
                zz = z[t % 2]
                pe.wait_ge(s_sTm, t + 1)
                pe.wait_ge(s_R, t + 1)
                for h in (0, 2, 1, 3):
                    b = 64 * (h % 2)
                    v = zz[:, CRV + h * 64:CRV + h * 64 + 64]
                    nc.tensor.matmul(oR[:, h * 64:h * 64 + 64], sTm[:, h, :], v, start=True, stop=False)
                    mm = nc.tensor.matmul(oR[:, h * 64:h * 64 + 64], k.rT[b:b + 64, 2 + h // 2, :], Rst[b:b + 64, h // 2, :],
                                          start=False, stop=True)
                    if h == 2:
                        mm.then_inc(s_row, 1)
                        pe.wait_ge(s_row, 2 * t + 2)
                for h in range(4):
                    b = 64 * (h % 2)
                    v = zz[:, CRV + h * 64:CRV + h * 64 + 64]
                    mm = nc.tensor.matmul(oR[b:b + 64, 256 + 64 * (h // 2):320 + 64 * (h // 2)], kz[:, h * 64:h * 64 + 64], v,
                                          start=True, stop=True)
                mm.then_inc(s_o, 1)

            pe.wait_ge(s_c, 16 * 12)
            pre(0)
            for t in range(NA):
                project(t)
            post(NA - 1, 2)

        @block.scalar
        def _(act):
            def pre(t):
                R = rows(t)
                act.wait_ge(s_x, 16 * (t + 1))
                if t >= 1:
                    act.wait_ge(s_xT, t)
                nc.scalar.activation(xs[:R, :], xb[:R, :], ACT.Square, accum_out=xss[:R, t:t + 1]).then_inc(s_xss, 1)
                act.wait_ge(s_xms, t + 1)
                nc.scalar.activation(xss[:R, 2 * NA + t:2 * NA + t + 1], xss[:R, NA + t:NA + t + 1], ACT.Sqrt).then_inc(s_xrt, 1)

            def evict_z(t):
                R, zz = rows(t), z[t % 2]
                for n, (c0, cn) in enumerate(slices(t)):
                    s = zs(t) + n
                    act.wait_ge(s_zmm, s + 1)
                    if n == 0 and t >= 2:
                        act.wait_ge(s_out[t % 2], stored(t - 2))
                        act.wait_ge(s_pool, t - 1)
                        if t - 2 < PT:
                            act.wait_ge(s_o, t - 1)
                        else:
                            act.wait_ge(s_pt, pg(t - 1))
                            act.wait_ge(s_rot, min(t - 1, NT))
                    nc.scalar.copy(zz[:R, c0:c0 + cn], zp[s % 2][:R, :cn]).then_inc(s_zev, 1)
                    if n == 0 and t + 1 < NA:
                        pre(t + 1)
                    for step in steps(t, n):
                        if t >= 1:
                            evict_post(t - 1, step)

            def squares(t):
                R, zz = rows(t), z[t % 2]
                act.wait_ge(s_zev, zs(t + 1))
                if t >= 1:
                    act.wait_ge(s_pt, pg(t - 1) + (2 if t - 1 < NT else 1))
                if t < NT:
                    nc.scalar.activation(nrm[:R, 0:512], zz[:R, CQ:CQ + 512], ACT.Square)
                    nc.scalar.activation(nrm[:R, 512:640], zz[:R, CKS:CKS + 128], ACT.Square)
                    nc.scalar.activation(nrm[:R, 640:768], zz[:R, CKW:CKW + 128], ACT.Square)
                    nc.scalar.activation(nrm[:R, 768:1024], zz[:R, CMQ:CMQ + 256], ACT.Square).then_inc(s_hsq, 1)
                else:
                    nc.scalar.activation(nrm[:, 0:256], zz[:, 0:256], ACT.Square).then_inc(s_hsq, 1)
                act.wait_ge(s_hms, t + 1)
                nc.scalar.activation(hss[:R, 1, :], hss[:R, 0, :], ACT.Sqrt).then_inc(s_hrt, 1)

            def evict_post(t, step):
                R = rows(t)
                tk = slice(t * P, t * P + R)
                g = pg(t)
                if step == 2:
                    act.wait_ge(s_pt, g + 1)
                    if t >= NT:
                        nc.scalar.copy(k.mkT[:, :, (t - NT) * P:(t - NT + 1) * P], pt[g % 2][:, 0:2, :]).then_inc(s_ptev, 1)
                        return
                    nc.scalar.activation(k.qT[:, :, tk], pt[g % 2][:, :, :R], ACT.Copy, scale=gq[:, 0:1]).then_inc(s_ptev, 1)
                    act.wait_ge(s_pt, g + 2)
                    q = pt[(g + 1) % 2]
                    nc.scalar.copy(k.ksT[:, tk], q[:, 0, :R])
                    nc.scalar.copy(k.kwT[:, tk], q[:, 1, :R])
                    nc.scalar.activation(k.mqT[:, :, tk], q[:, 2:4, :R], ACT.Copy, scale=gq[:, 1:2]).then_inc(s_ptev, 1)
                if step == 3 and t < NT:
                    act.wait_ge(s_pt, g + 3)
                    nc.scalar.copy(k.rT[:, 0:4, :R], pt[g % 2][:, :, :R]).then_inc(s_ptev, 1)
                    act.wait_ge(s_pt, g + 4)
                    nc.scalar.copy(k.rT[:, 4:6, :R], pt[(g + 1) % 2][:, 0:2, :R]).then_inc(s_ptev, 1)

            act.wait_ge(s_g0, 1)
            pre(0)
            for t in range(NA):
                if t >= 1:
                    squares(t - 1)
                evict_z(t)
            squares(NA - 1)
            evict_post(NA - 1, 2)

        @block.vector
        def _(dve):
            n_dc = [0]

            def link(ins):
                n_dc[0] += 1
                ins.then_inc(s_dc, 1)
                dve.wait_ge(s_dc, n_dc[0])

            def pre(t):
                R = rows(t)
                dve.wait_ge(s_xss, t + 1)
                nc.vector.tensor_scalar(xss[:R, NA + t:NA + t + 1], xss[:R, t:t + 1], 1.0 / D, EPS, ALU.mult, ALU.add).then_inc(s_xms, 1)
                dve.wait_ge(s_xrt, t + 1)
                link(nc.vector.reciprocal(xss[:R, 3 * NA + t:3 * NA + t + 1], xss[:R, 2 * NA + t:2 * NA + t + 1]))
                nc.vector.tensor_scalar(xs[:R, :], xb[:R, :], xss[:R, 3 * NA + t:3 * NA + t + 1], None, ALU.mult).then_inc(s_xs, 1)
                dve.wait_ge(s_xT, t + 1)
                if t >= 2:
                    dve.wait_ge(s_zmm, zs(t - 1))
                for h in range(2):
                    nc.vector.tensor_tensor(xnT[t % 2][:, 4 * h:4 * h + 4, :R], xT[h][:, :, :R],
                                            bc(gx[:, 0 if t < NT else 1, 4 * h:4 * h + 4], R), ALU.mult).then_inc(s_xnT, 1)

            def norm(t):
                R, zz = rows(t), z[t % 2]
                dve.wait_ge(s_hsq, t + 1)
                nh = 16 if t < NT else 4
                link(nc.vector.tensor_reduce(hss[:R, 0, :nh], nrm[:R, :64 * nh].rearrange("p (h d) -> p h d", d=64), AX.X, ALU.add))
                nc.vector.tensor_scalar(hss[:R, 0, :], hss[:R, 0, :], 1.0 / HD, EPS, ALU.mult, ALU.add).then_inc(s_hms, 1)
                dve.wait_ge(s_hrt, t + 1)
                link(nc.vector.reciprocal(hss[:R, 1, :], hss[:R, 1, :]))
                r = hss[:, 1, :]
                heads = lambda ap: ap.rearrange("p (h d) -> p h d", d=64)

                def scaled(out, src, j, n):
                    return nc.vector.tensor_tensor(out, heads(src), bc(r[:R, j:j + n], 64), ALU.mult)

                def gained(z0, src, j, n):
                    gb = ghead[:R, j, :].unsqueeze(1).broadcast_to([R, n, 64])
                    return nc.vector.tensor_tensor(heads(zz[:R, z0:z0 + 64 * n]), heads(src), gb, ALU.mult)

                if t >= NT:
                    link(scaled(heads(nrm[:R, 0:256]), zz[:R, 0:256], 0, 4))
                    gained(0, nrm[:R, 0:256], 2, 4).then_inc(s_nrm, 1)
                    return
                qo = nrm[:R, 0:512].rearrange("p (c g d) -> p g c d", c=4, g=2)
                scaled(heads(nrm[:R, 512:640]), zz[:R, CKS:CKS + 128], 8, 2)
                link(scaled(heads(nrm[:R, 640:768]), zz[:R, CKW:CKW + 128], 10, 2))
                for g in range(2):
                    scaled(qo[:, g], zz[:R, CQ + 256 * g:CQ + 256 * g + 256], 4 * g, 4)
                scaled(heads(nrm[:R, 768:1024]), zz[:R, CMQ:CMQ + 256], 12, 4)
                gained(CKS, nrm[:R, 512:640], 0, 2)
                gained(CKW, nrm[:R, 640:768], 1, 2).then_inc(s_nrm, 1)
                if t >= 1:
                    dve.wait_ge(s_pt, pg(t))
                    dve.wait_ge(s_o, t)
                src = zz[:R, CRQ:CRQ + 512].rearrange("p (h x) -> p h x", x=32)
                cs = lambda n: C[:R, at[n]].rearrange("p (t x) -> p t x", x=32)[:, t, :].unsqueeze(1).broadcast_to([R, 16, 32])
                nc.vector.tensor_tensor(tr[:R, 0, :].rearrange("p (h x) -> p h x", x=32), src, cs("cos"), ALU.mult)
                link(nc.vector.tensor_tensor(tr[:R, 1, :].rearrange("p (h x) -> p h x", x=32), src, cs("sin"), ALU.mult))
                v4 = lambda ap: ap.rearrange("p (h y x) -> p h y x", y=2, x=32)
                c4, s4, r4 = v4(tr[:R, 0, :]), v4(tr[:R, 1, :]), v4(rot[:R, :])
                nc.vector.tensor_tensor(r4[:, :, 0, :], c4[:, :, 0, :], s4[:, :, 1, :], ALU.subtract)
                link(nc.vector.tensor_tensor(r4[:, :, 1, :], s4[:, :, 0, :], c4[:, :, 1, :], ALU.add))
                kind = 0 if t < PT else 1
                nc.vector.tensor_tensor(heads(qxi[:R, :]), heads(rot[:R, 0:256]),
                                        bc(C[:R, at["xi"]][:, 4 * kind:4 * kind + 4], 64), ALU.mult)
                nc.vector.tensor_tensor(heads(kz[:R, :]), heads(rot[:R, 256:512]),
                                        bc(C[:R, at["zeta"]][:, 4 * kind:4 * kind + 4], 64), ALU.mult).then_inc(s_rot, 1)

            def retention(t):
                dve.wait_ge(s_sT, t + 1)
                nc.vector.tensor_tensor(sTm[:], sTp[:], C[:, at["dmaskT"]].rearrange("p (h n) -> p h n", h=4), ALU.mult).then_inc(s_sTm, 1)
                dve.wait_ge(s_o, t + 1)
                nc.vector.tensor_copy(k.oret[:, t, :], oR[:, 0:256])
                for pair in range(2):
                    ins = nc.vector.scalar_tensor_tensor(out=Rst[:, pair, :], in0=Rst[:, pair, :],
                                                         scalar=C[:, at["decay"]][:, pair:pair + 1],
                                                         in1=oR[:, 256 + 64 * pair:320 + 64 * pair], op0=ALU.mult, op1=ALU.add)
                ins.then_inc(s_R, 1)

            nc.vector.memset(hss[:], 1.0)
            nc.vector.memset(Rst[:], 0.0).then_inc(s_R, 1)
            dve.wait_ge(s_c, 16 * 12)
            nc.vector.tensor_scalar(gq[:], gq[:], HD ** -0.5, None, ALU.mult).then_inc(s_g0, 1)
            pre(0)
            for t in range(NA):
                if t >= 1:
                    norm(t - 1)
                if t + 1 < NA:
                    pre(t + 1)
                if 1 <= t <= PT:
                    retention(t - 1)
            norm(NA - 1)


def phase_compress(nc, k):
    i, o, at, C, B = k.i, k.o, k.at, k.C, k.B
    SRC = [(8, 1), (0, 4), (4, 4)]
    SEQ = [("T", 0, 0), ("T", 0, 1), ("M", 0, 0), ("T", 1, 0), ("S", 0, 0), ("M", 0, 1), ("N", 0, 0), ("T", 1, 1),
           ("S", 0, 1), ("M", 1, 0), ("T", 2, 0), ("S", 1, 0), ("M", 1, 1), ("N", 1, 0), ("T", 2, 1), ("S", 1, 1),
           ("M", 2, 0), ("S", 2, 0), ("M", 2, 1), ("N", 2, 0), ("S", 2, 1)]
    with ExitStack() as ctx:
        sb = lambda n, s, d=F32: ctx.enter_context(nc.sbuf_tensor(n, s, d))
        ps = lambda n, s, d=F32: ctx.enter_context(nc.psum_tensor(n, s, d))
        sem = k.sem
        x2 = sb("x2", [P, 4, 4, 4, P])
        xT = [sb(f"x2T{j}", [P, 4, G, 512]) for j in range(2)]
        w1 = [sb(f"w1{j}", [P, 16, HID]) for j in range(2)]
        w2 = sb("w2", [P, 2, 2, HD])
        pe_c = sb("pe_c", [P, 2, 16])
        gkc = sb("gkc", [P, 1])
        bias = sb("cbias", [P, 4])
        hid_all = sb("hid", [P, 4 * 4 * P])
        hid = hid_all[:, 0:2 * 2 * 504].rearrange("p (a b n) -> p a b n", a=2, b=2)
        x2_of = [hid_all[:].rearrange("p (e t a x) -> p e t a x", e=1, t=4, a=4), x2, x2]
        raw, sq, rt = sb("kc_raw", [P, 252]), sb("kc_sq", [P, 252]), sb("kc_rt", [P, 252])
        tp = [ps(f"ctp{j}", [P, 4, P]) for j in range(3)]
        acc = [ps(f"cacc{j}", [P, 512]) for j in range(2)]
        kcp, vcp, bp = ps("kcp", [P, 512]), ps("vcp", [P, 512]), ps("cbp", [P, 4])
        s_w = [sem(f"cmp_w_loaded{j}") for j in range(2)]
        s_s, s_x = sem("cmp_small_loaded"), [sem(f"pairs_loaded{j}") for j in range(3)]
        s_xo = [None] + [sem(f"pool_pairs_loaded{j}") for j in range(2)]
        s_t, s_te = sem("pairs_transposed"), [sem("pairs_evicted_dve"), sem("pairs_evicted_act")]
        s_b, s_be = sem("pe_bias_done"), sem("pe_bias_evicted")
        s_m, s_g = sem("hidden_done"), sem("gelu_done")
        s_k, s_v = sem("kc_done"), sem("vc_done")
        s_raw, s_sq, s_mean, s_ms, s_rt, s_kc, s_vc = (sem("kc_raw_copied"), sem("kc_squared"), sem("kc_mean_done"),
            sem("kc_mean_square"), sem("kc_root"), sem("kc_ready"), sem("vc_ready"))
        s_dc = sem("cmp_dve_chain")
        first_t, first_m, nt_, nm_ = {}, {}, 0, 0
        for op, gi, kv in SEQ:
            if op == "T":
                first_t[gi, kv] = nt_
                nt_ += SRC[gi][1] * G
            if op == "M":
                first_m[gi, kv] = nm_
                nm_ += 2
        nT = lambda gi: SRC[gi][1] * G
        done_by = lambda n, e: (n + 1 - e) // 2
        block = ctx.enter_context(nc.Block())

        def load_pages(eng, gi, pool):
            b0, nb = SRC[gi]
            for b in range(nb):
                for pg in range(PAGES):
                    if (pg in POOL_PAGES) != pool:
                        continue
                    n = (b0 + b) * PAGES + pg
                    page = eng.value_load(k.pages[0:1, n:n + 1], min_val=0, max_val=i["cache_cmp_kv"].shape[1] - 1)
                    src = i["cache_cmp_kv"][0, bass.ds(page, 1)].rearrange("o (m r) k g d -> (o m) r (k g) d", r=2)
                    h = 64 * (pg % 2)
                    dst = x2[h:h + 64, b, pg // 2].rearrange("p a (r d) -> p r a d", r=2)
                    for r in range(2):
                        eng.dma_start(dst[:, r], src[:, r]).then_inc((s_x, s_xo)[pool][gi], 16)

        @block.sync
        def _(sp):
            prompt = o["cmp_p"].rearrange("l b (t m r) k g d -> (l b m) t r (k g) d", m=P, r=2)
            for jt in range(4):
                for r in range(2):
                    sp.dma_start(x2_of[0][:, 0, jt].rearrange("p a (r d) -> p r a d", r=2)[:, r], prompt[:, jt, r]).then_inc(s_x[0], 16)
            load_pages(sp, 1, False)
            for j, n in enumerate(("k", "v")):
                sp.dma_start(w2[:, j], i[f"cmp_w2_{n}"][0].rearrange("(c p) d -> p c d", p=P)).then_inc(s_s, 16)
            sp.dma_start(B[:], i["tables_b"]).then_inc(s_s, 16)
            sp.wait_ge(s_t, first_t[1, 1] + nT(1))
            load_pages(sp, 2, False)

        @block.gpsimd
        def _(pool):
            pool.wait_ge(s_w[0], 32)
            load_pages(pool, 1, True)
            pool.wait_ge(s_t, first_t[1, 1] + nT(1))
            load_pages(pool, 2, True)

        @block.scalar
        def _(act):
            with nc.allow_non_contiguous_dma(reason="position encodings and gain, small"):
                for j, n in enumerate(("k", "v")):
                    act.dma_start(w1[j][:], i[f"cmp_w1_{n}"][0].rearrange("(c p) h -> p c h", p=P)).then_inc(s_w[j], 16)
                    act.dma_start(pe_c[:, j, :], i[f"cmp_pe_{n}"][0].rearrange("(c r) d -> (r d) c", r=2)).then_inc(s_w[j], 16)
                for half in range(2):
                    act.dma_start(gkc[64 * half:64 * half + 64, :], i["k_norm_cmp_g"].rearrange("l d -> d l")).then_inc(s_s, 16)
            for op, gi, kv in SEQ:
                nb = SRC[gi][1]
                if op == "T":
                    for m in range(nT(gi)):
                        n = first_t[gi, kv] + m
                        if n % 2 == 1:
                            act.wait_ge(s_t, n + 1)
                            if gi >= 1:
                                act.wait_ge(s_m, first_m[gi - 1, kv] + 2)
                            nc.scalar.copy(xT[kv][:, m // G, m % G, :], tp[n % 3][:].rearrange("p a b -> p (a b)")).then_inc(s_te[1], 1)
                if op == "M":
                    if gi == 0:
                        act.wait_ge(s_be, kv + 1)
                    if gi >= 1:
                        act.wait_ge((s_k, s_v)[kv], gi)
                    for hh in range(2):
                        n = first_m[gi, kv] + hh
                        act.wait_ge(s_m, n + 1)
                        nc.scalar.activation(hid[:, kv, hh, :nb * 126], acc[n % 2][:, :nb * 126], ACT.Gelu_apprx_tanh,
                                             bias=bias[:, 2 * kv + hh:2 * kv + hh + 1]).then_inc(s_g, 1)
                if op == "N":
                    nn = nb * NCMP
                    act.wait_ge(s_raw, gi + 1)
                    nc.scalar.activation(sq[:, :nn], raw[:, :nn], ACT.Square).then_inc(s_sq, 1)
                    act.wait_ge(s_ms, gi + 1)
                    nc.scalar.activation(rt[:, :nn], rt[:, :nn], ACT.Sqrt).then_inc(s_rt, 1)

        @block.tensor
        def _(pe):
            ident = C[:, at["ident"]]
            for op, gi, kv in SEQ:
                b0, nb = SRC[gi]
                if op == "T":
                    if kv == 0:
                        npool = 2 * nb * len(POOL_PAGES)
                        pe.wait_ge(s_x[gi], 16 * (2 * nb * PAGES - npool if gi else 8))
                        if gi:
                            pe.wait_ge(s_xo[gi], 16 * npool)
                    for m in range(nT(gi)):
                        n = first_t[gi, kv] + m
                        if n >= 3:
                            for e in range(2):
                                pe.wait_ge(s_te[e], done_by(n - 2, e))
                        for jt in range(4):
                            mm = nc.tensor.transpose(tp[n % 3][:, jt, :], x2_of[gi][:, m // G, jt, kv * G + m % G, :], ident)
                        mm.then_inc(s_t, 1)
                if op == "M":
                    if gi == 0:
                        pe.wait_ge(s_w[kv], 32)
                        for hh in range(2):
                            for jj in range(16):
                                mm = nc.tensor.matmul(bp[:, 2 * kv + hh:2 * kv + hh + 1], w1[kv][:, jj, hh * P:hh * P + P],
                                                      pe_c[:, kv, jj:jj + 1], start=(jj == 0), stop=(jj == 15))
                        mm.then_inc(s_b, 1)
                    n_t = first_t[gi, kv] + nT(gi)
                    for e in range(2):
                        pe.wait_ge(s_te[e], done_by(n_t, e))
                    for hh in range(2):
                        n = first_m[gi, kv] + hh
                        if n >= 2:
                            pe.wait_ge(s_g, n - 1)
                        for jj in range(16):
                            rhs = xT[kv][:, :nb].rearrange("p b g m -> p (b g) m")[:, :, jj:jj + 8 * NCMP - 7:8]
                            mm = nc.tensor.matmul(acc[n % 2][:, :nb * 126].rearrange("p (b n) -> p b n", n=NCMP),
                                                  w1[kv][:, jj, hh * P:hh * P + P], rhs, start=(jj == 0), stop=(jj == 15))
                        mm.then_inc(s_m, 1)
                if op == "S":
                    pe.wait_ge(s_g, first_m[gi, kv] + 2)
                    if gi == 0 and kv == 0:
                        pe.wait_ge(s_s, 16 * 5)
                    h4 = lambda hh: hid[:, kv, hh, :nb * 126].rearrange("p (b g n) -> p g b n", g=G, n=NCMP)
                    if kv == 0:
                        if gi >= 1:
                            pe.wait_ge(s_kc, gi)
                        for g in range(G):
                            for hh in range(2):
                                mm = nc.tensor.matmul(kcp[64 * g:64 * g + 64, :nb * NCMP].rearrange("p (b n) -> p b n", n=NCMP),
                                                      w2[:, 0, hh, :], h4(hh)[:, g], start=(hh == 0), stop=(hh == 1))
                        mm.then_inc(s_k, 1)
                    else:
                        if gi >= 1:
                            pe.wait_ge(s_vc, gi)
                        for b in range(nb):
                            for g in range(G):
                                for hh in range(2):
                                    mm = nc.tensor.matmul(vcp[:NCMP, (b * G + g) * HD:(b * G + g + 1) * HD],
                                                          h4(hh)[:, g, b, :], w2[:, 1, hh, :], start=(hh == 0), stop=(hh == 1))
                        mm.then_inc(s_v, 1)
                if op == "N":
                    pe.wait_ge(s_sq, gi + 1)
                    nc.tensor.matmul(kcp[:, 256:256 + nb * NCMP], B[:, at["blockmean"]], sq[:, :nb * NCMP],
                                     start=True, stop=True).then_inc(s_mean, 1)

        @block.vector
        def _(dve):
            n_dc = [0]

            def link(ins):
                n_dc[0] += 1
                ins.then_inc(s_dc, 1)
                dve.wait_ge(s_dc, n_dc[0])

            for op, gi, kv in SEQ:
                b0, nb = SRC[gi]
                nn = nb * NCMP
                if op == "T":
                    for m in range(nT(gi)):
                        n = first_t[gi, kv] + m
                        if n % 2 == 0:
                            dve.wait_ge(s_t, n + 1)
                            if gi >= 1:
                                dve.wait_ge(s_m, first_m[gi - 1, kv] + 2)
                            nc.vector.tensor_copy(xT[kv][:, m // G, m % G, :], tp[n % 3][:].rearrange("p a b -> p (a b)")).then_inc(s_te[0], 1)
                if op == "M" and gi == 0:
                    dve.wait_ge(s_b, kv + 1)
                    nc.vector.tensor_copy(bias[:, 2 * kv:2 * kv + 2], bp[:, 2 * kv:2 * kv + 2]).then_inc(s_be, 1)
                if op == "S" and kv == 0:
                    dve.wait_ge(s_k, gi + 1)
                    nc.vector.tensor_copy(raw[:, :nn], kcp[:, :nn]).then_inc(s_raw, 1)
                if op == "S" and kv == 1:
                    dve.wait_ge(s_v, gi + 1)
                    nc.vector.tensor_copy(k.vc[:, b0:b0 + nb, :], vcp[:NCMP, :nb * P].rearrange("p (b x) -> p b x", b=nb)).then_inc(s_vc, 1)
                if op == "N":
                    dve.wait_ge(s_mean, gi + 1)
                    nc.vector.tensor_scalar(rt[:, :nn], kcp[:, 256:256 + nn], EPS, None, ALU.add).then_inc(s_ms, 1)
                    dve.wait_ge(s_rt, gi + 1)
                    link(nc.vector.reciprocal(rt[:, :nn], rt[:, :nn]))
                    nc.vector.scalar_tensor_tensor(out=k.kcT[:, b0:b0 + nb, :].rearrange("p b n -> p (b n)"), in0=raw[:, :nn], scalar=gkc[:, 0:1],
                                                   in1=rt[:, :nn], op0=ALU.mult, op1=ALU.mult).then_inc(s_kc, 1)


def phase_prompt(nc, k):
    i, o, at, C, B = k.i, k.o, k.at, k.C, k.B
    HU, GROUPS = [], []
    for qt in range(PT):
        for g in range(G):
            for c in range(HPG):
                HU += [("W", qt, g, c), ("L", qt, g, c)]
            GROUPS.append((qt, g, len(HU) - 1))
        HU.append(("M", qt, 2, 0))
        GROUPS.append((qt, 2, len(HU) - 1))
    win = lambda qt: list(range(max(0, qt - 4), qt + 1))

    def steps_of(n):
        qt, g, _ = GROUPS[n]
        if g == 2:
            return [(n, "M", 0, 0), (n, "M", 1, 1)]
        return ([(n, "L", kt, kt) for kt in range(qt + 1)] + [(n, "W", kt, j) for j, kt in enumerate(win(qt))]
                + [(n, "C", 0, 0)])

    STEPS, AT = [], [[] for _ in range(len(HU) + 1)]
    for n in range(len(GROUPS)):
        st = steps_of(n)
        first, span = (GROUPS[n][2] + 2, 7) if GROUPS[n][1] < 2 else (GROUPS[n][2] + 8, 1)
        for j, x in enumerate(st):
            AT[min(len(HU), first + j * span // len(st))].append(len(STEPS))
            STEPS.append(x)
    last_step = {}
    for x, st in enumerate(STEPS):
        last_step[st[0]] = x
    with ExitStack() as ctx:
        sb = lambda n, s, d=F32: ctx.enter_context(nc.sbuf_tensor(n, s, d))
        ps = lambda n, s, d=F32: ctx.enter_context(nc.psum_tensor(n, s, d))
        sem = k.sem
        identb, causb, winb = sb("ident_b", [P, P], BF16), sb("causal_b", [P, P], BF16), sb("winlow_b", [P, P], BF16)
        cmpb = sb("cmpmask_b", [P, PT, NCMP], BF16)
        Pb = [sb(f"P{j}", [P, 4, 1728]) for j in range(2)]
        Pb.append(sb("Pmem", [P, 4, 256]))
        pbuf = lambda qt, g: Pb[2 if g == 2 else g]
        PTs = [sb(f"PTs{j}", [P, 512]) for j in range(2)]
        nm, den, rs = sb("neg_max", [P, 4, 4]), sb("den", [P, 4, 4]), sb("p_scale", [P, 4, 4])
        sc = [ps(f"scores{j}", [P, 1024]) for j in range(2)]
        ptp = [ps(f"PTp{j}", [P, 4, P]) for j in range(2)]
        op = [ps(f"attn_out{j}", [P, 512]) for j in range(2)]
        s_m, s_sg = sem("masks_ready"), sem("gates_ready")
        s_sc, s_nm, s_ex, s_p = sem("scores_done"), sem("neg_max_ready"), sem("exp_done"), sem("p_scaled")
        s_t, s_te = sem("p_transposed"), [sem("pT_evicted_dve"), sem("pT_evicted_act")]
        s_pv, s_o = sem("value_step_done"), sem("attn_out_copied")
        s_dc, s_out, s_z = sem("prompt_dve_chain"), sem("ret_state_stored"), sem("zero_ready")
        zero = sb("zero", [P, D])
        done_by = lambda n, e: (n + 1 - e) // 2
        block = ctx.enter_context(nc.Block())

        @block.sync
        def _(sp):
            sp.dma_start(o["ret_p"].rearrange("l b (i a) d e -> (l b a d) i e", a=2), k.Rst[:]).then_inc(s_out, 16)
            sp.wait_ge(s_z, 1)
            sp.dma_start(k.y_dram[CAP * NE:NSLOT, :].rearrange("(b p) d -> p b d", p=P),
                         zero[:].unsqueeze(1).broadcast_to([P, (NSLOT - CAP * NE) // P, D])).then_inc(s_out, 16)
            sp.wait_ge(s_out, 32)

        @block.gpsimd
        def _(pool):
            nc.gpsimd.memset(zero[:], 0.0).then_inc(s_z, 1)

        def scores(pe, x):
            kind, qt, g, c = HU[x]
            q = slice(qt * P, qt * P + P)
            t = sc[x % 2]
            if x >= 2:
                pe.wait_ge(s_ex, x - 1)
            mask = lambda out, m, stop=True: nc.tensor.matmul(out, identb[:], m, start=False, stop=stop)
            if kind == "M":
                for h in (0, 2, 1, 3):
                    b = 64 * (h % 2)
                    c0 = 512 * (h % 2) + 256 * (h // 2)
                    mm = nc.tensor.matmul(t[:, c0:c0 + 256], k.mqT[b:b + 64, h // 2, q], k.mkT[b:b + 64, h // 2, :],
                                          start=True, stop=True)
            else:
                b = 64 * g
                lhs = k.qT[b:b + 64, c, q]
                kT, tiles = (k.ksT, list(range(qt + 1))) if kind == "L" else (k.kwT, win(qt))
                for c0 in range(0, len(tiles), 4):
                    part = tiles[c0:c0 + 4]
                    low = kind == "W" and qt >= 4 and c0 == 0
                    diag = part[-1] == qt
                    mm = nc.tensor.matmul(t[:, c0 * P:(c0 + len(part)) * P], lhs, kT[b:b + 64, part[0] * P:(part[-1] + 1) * P],
                                          start=True, stop=not (low or diag))
                    if low:
                        mm = mask(t[:, 0:P], winb[:], stop=not diag)
                    if diag:
                        e = (c0 + len(part)) * P
                        mm = mask(t[:, e - P:e], causb[:])
                if kind == "W":
                    nc.tensor.matmul(t[:, 640:640 + NCMP], lhs, k.kcT[b:b + 64, DB, :], start=True, stop=False)
                    mm = mask(t[:, 640:640 + NCMP], cmpb[:, qt, :])
            mm.then_inc(s_sc, 1)

        def psrc(x, h):
            n, kind, kt, j = STEPS[x]
            p = pbuf(*GROUPS[n][:2])[:, h, :]
            if kind == "L":
                return p[:, j * P:j * P + P]
            if kind == "W":
                return p[:, 1024 + j * P:1024 + j * P + P]
            if kind == "M":
                return p[:, j * P:j * P + P]
            return p[:, 1664:1664 + NCMP]

        @block.tensor
        def _(pe):
            ident = C[:, at["ident"]]

            def turn(x):
                n, kind, _, _ = STEPS[x]
                pe.wait_ge(s_p, GROUPS[n][2] + 1)
                if x >= 2:
                    pe.wait_ge(s_te[x % 2], done_by(x - 1, x % 2))
                w = NCMP if kind == "C" else P
                for h in range(4):
                    mm = nc.tensor.transpose(ptp[x % 2][:w, h, :], psrc(x, h), ident)
                mm.then_inc(s_t, 1)

            def values(x):
                n, kind, kt, j = STEPS[x]
                qt, g, _ = GROUPS[n]
                first = x == 0 or STEPS[x - 1][0] != n
                last = last_step[n] == x
                pe.wait_ge(s_te[x % 2], done_by(x + 1, x % 2))
                if first and n >= 2:
                    pe.wait_ge(s_o, n - 1)
                ob = op[n % 2]
                if kind == "M":
                    if j == 0:
                        return
                    pe.wait_ge(s_te[(x - 1) % 2], done_by(x, (x - 1) % 2))
                    for h in range(4):
                        b = 64 * (h % 2)
                        for m in range(2):
                            mm = nc.tensor.matmul(ob[b:b + 64, (h // 2) * P:(h // 2 + 1) * P], k.mv[:, m, h * 64:h * 64 + 64],
                                                  PTs[(x - 1 + m) % 2][:, h * P:h * P + P], start=(m == 0), stop=(m == 1))
                    mm.then_inc(s_pv, 2)
                    return
                b = 64 * g
                if kind == "C":
                    v, rhs = k.vc[:, DB, b:b + 64], PTs[x % 2][:NCMP, :]
                else:
                    v, rhs = (k.vs if kind == "L" else k.vw)[:, kt, b:b + 64], PTs[x % 2][:]
                nc.tensor.matmul(ob[b:b + 64, :], v, rhs, start=first, stop=last).then_inc(s_pv, 1)

            pe.wait_ge(s_m, 1)
            for x in range(len(HU) + 1):
                if x < len(HU):
                    scores(pe, x)
                for y in AT[x]:
                    turn(y)
                    if y >= 1:
                        values(y - 1)
            values(len(STEPS) - 1)

        def evict(eng, op_copy, y, e):
            n, kind, _, _ = STEPS[y]
            w = NCMP if kind == "C" else P
            eng.wait_ge(s_t, y + 1)
            if y >= 2:
                eng.wait_ge(s_pv, y - 1)
            op_copy(PTs[e][:w, :], ptp[e][:w].rearrange("p a b -> p (a b)")).then_inc(s_te[e], 1)

        @block.scalar
        def _(act):
            nc.scalar.activation(k.gate[:, 0:PT, :], k.gate[:, 0:PT, :], ACT.Sigmoid).then_inc(s_sg, 1)
            nc.scalar.activation(k.gate[:SR, PT, :], k.gate[:SR, PT, :], ACT.Sigmoid).then_inc(s_sg, 1)
            for x in range(len(HU) + 1):
                if x < len(HU):
                    kind, qt, g, c = HU[x]
                    n = 3 * qt + g
                    t, r = sc[x % 2], x % 4
                    pb = pbuf(qt, g)
                    act.wait_ge(s_nm, x + 1)
                    if n >= 3:
                        act.wait_ge(s_t, last_step[n - 3] + 1)
                    if x >= 4:
                        act.wait_ge(s_p, x - 3)
                    if kind == "M":
                        for h in range(4):
                            c0 = 512 * (h % 2) + 256 * (h // 2)
                            ins = nc.scalar.activation(pb[:, h, 0:256], t[:, c0:c0 + 256], ACT.Exp, bias=nm[:, r, h:h + 1],
                                                       accum_out=den[:, r, h:h + 1])
                    elif kind == "L":
                        w = (qt + 1) * P
                        ins = nc.scalar.activation(pb[:, c, 0:w], t[:, 0:w], ACT.Exp, bias=nm[:, r, 0:1], accum_out=den[:, r, 0:1])
                    else:
                        w = len(win(qt)) * P
                        nc.scalar.activation(pb[:, c, 1024:1024 + w], t[:, 0:w], ACT.Exp, bias=nm[:, r, 0:1], accum_out=den[:, r, 0:1])
                        ins = nc.scalar.activation(pb[:, c, 1664:1664 + NCMP], t[:, 640:640 + NCMP], ACT.Exp, bias=nm[:, r, 1:2],
                                                   accum_out=den[:, r, 1:2])
                    ins.then_inc(s_ex, 1)
                for y in AT[x]:
                    if y % 2 == 1:
                        evict(act, nc.scalar.copy, y, 1)

        @block.vector
        def _(dve):
            n_dc = [0]

            def link(ins):
                n_dc[0] += 1
                ins.then_inc(s_dc, 1)
                dve.wait_ge(s_dc, n_dc[0])

            def maxima(x):
                kind, qt, g, c = HU[x]
                t, r = sc[x % 2], x % 4
                dve.wait_ge(s_sc, x + 1)
                if x >= 4:
                    dve.wait_ge(s_ex, x - 3)
                red = lambda out, src: nc.vector.tensor_reduce(out, src, AX.X, ALU.max, negate=True)
                if kind == "M":
                    ins = red(nm[:, r, :].rearrange("p (i a) -> p a i", a=2), t[:].rearrange("p (a i n) -> p a i n", a=2, i=2))
                elif kind == "L":
                    ins = red(nm[:, r, 0:1], t[:, 0:(qt + 1) * P])
                else:
                    red(nm[:, r, 0:1], t[:, 0:len(win(qt)) * P])
                    ins = red(nm[:, r, 1:2], t[:, 640:640 + NCMP])
                ins.then_inc(s_nm, 1)

            def scale(x):
                kind, qt, g, c = HU[x]
                r, pb = x % 4, pbuf(qt, g)
                dve.wait_ge(s_ex, x + 1)
                gt = lambda br: k.gate[:, qt, (g * 4 + c) * 3 + br:(g * 4 + c) * 3 + br + 1]
                if kind == "M":
                    link(nc.vector.reciprocal(rs[:, r, :], den[:, r, :]))
                    ins = nc.vector.tensor_tensor(pb[:, :, 0:256], pb[:, :, 0:256], bc(rs[:, r, :], 256), ALU.mult)
                elif kind == "L":
                    link(nc.vector.reciprocal(rs[:, r, 0:1], den[:, r, 0:1]))
                    ins = nc.vector.tensor_scalar(pb[:, c, 0:(qt + 1) * P], pb[:, c, 0:(qt + 1) * P], rs[:, r, 0:1], gt(1),
                                                  ALU.mult, ALU.mult)
                else:
                    w = len(win(qt)) * P
                    link(nc.vector.reciprocal(rs[:, r, 0:2], den[:, r, 0:2]))
                    if qt == 0:
                        link(nc.vector.tensor_scalar(rs[:, r, 1:2], rs[:, r, 1:2], B[:, at["anycmp"]], None, ALU.mult))
                    nc.vector.tensor_scalar(pb[:, c, 1024:1024 + w], pb[:, c, 1024:1024 + w], rs[:, r, 0:1], gt(2), ALU.mult, ALU.mult)
                    ins = nc.vector.tensor_scalar(pb[:, c, 1664:1664 + NCMP], pb[:, c, 1664:1664 + NCMP], rs[:, r, 1:2], gt(0),
                                                  ALU.mult, ALU.mult)
                ins.then_inc(s_p, 1)

            def output(n):
                qt, g, _ = GROUPS[n]
                q = slice(qt * P, qt * P + P)
                dve.wait_ge(s_pv, last_step[n] + 1)
                if g == 2:
                    nc.vector.tensor_copy(k.mixT[:, 6:8, q], op[n % 2][:, 0:256].rearrange("p (i x) -> p i x", i=2)).then_inc(s_o, 1)
                else:
                    b = 64 * g
                    nc.vector.tensor_copy(k.mixT[b:b + 64, 0:4, q], op[n % 2][b:b + 64, :].rearrange("p (c x) -> p c x", c=4)).then_inc(s_o, 1)

            nc.vector.tensor_copy(identb[:], C[:, at["ident"]])
            nc.vector.tensor_copy(causb[:], B[:, at["causal"]])
            nc.vector.tensor_copy(winb[:], B[:, at["winlow"]])
            nc.vector.tensor_copy(cmpb[:], B[:, at["cmpmask"]].rearrange("p (t n) -> p t n", t=PT)).then_inc(s_m, 1)
            dve.wait_ge(s_sg, 2)
            copied = 0
            for x in range(len(HU) + 1):
                if x < len(HU):
                    maxima(x)
                if x >= 1:
                    scale(x - 1)
                for y in AT[x]:
                    if y % 2 == 0:
                        evict(dve, nc.vector.tensor_copy, y, 0)
                    while copied < len(GROUPS) and last_step[copied] < y:
                        output(copied)
                        copied += 1
            while copied < len(GROUPS):
                output(copied)
                copied += 1


def load_caches(eng, k, st, pool):
    for b in range(DB // 2):
        bb = DB // 2 * st + b
        for pg in range(PAGES):
            if (pg in POOL_PAGES) != pool:
                continue
            n = bb * PAGES + pg
            page = eng.value_load(k.pages[0:1, n:n + 1], min_val=0, max_val=k.i["cache_slc_kv"].shape[1] - 1)
            src = k.i["cache_slc_kv"][0, bass.ds(page, 1)].rearrange("o t k g d -> (o t) (k g d)")
            eng.dma_start(k.nat[:, b, pg, :], src).then_inc((k.s_cache, k.s_cache_pool)[pool][st], 16)
        if not pool:
            w = k.i["cache_win_kv"][0, bb].rearrange("(m p) k g d -> p m (k g d)", p=P)
            eng.dma_start(k.natw[:, b], w).then_inc(k.s_cache[st], 16)


def load_w_out(sp, k):
    wv = k.i["w_out"][0]
    for half in range(2):
        c0 = slice(half * 512, half * 512 + 512)
        for c in range(4):
            for g in range(G):
                r0 = (4 * g + c) * HD
                sp.dma_start(k.w_out[64 * g:64 * g + 64, c, c0], wv[r0:r0 + HD, c0]).then_inc(k.s_w_out[half], 16)
        sp.dma_start(k.w_out[:, 4:8, c0], wv[512:1024, c0].rearrange("(c p) n -> p c n", p=P)).then_inc(k.s_w_out[half], 16)


def phase_sample(nc, k):
    i, o, at, C, B = k.i, k.o, k.at, k.C, k.B
    NB = DB // 2
    SL, NS, WN, NW, CM = 0, 1024, 1056, 1568, 1600
    with ExitStack() as ctx:
        sb = lambda n, s, d=F32: ctx.enter_context(nc.sbuf_tensor(n, s, d))
        ps = lambda n, s, d=F32: ctx.enter_context(nc.psum_tensor(n, s, d))
        sem = k.sem
        nat, natw, s_x = k.nat, k.natw, k.s_cache
        flat = lambda t: t[:].rearrange("p t x -> p (t x)")
        nat_m = [flat(t)[:, n * 1024:n * 1024 + 1024].rearrange("p (m x) -> p m x", m=MT) for t in (k.rg, k.oret) for n in range(2)]
        nat_m += [t[:, 0:S].rearrange("p (m x) -> p m x", m=MT) for t in (k.ksT, k.kwT)]
        nat_m += [flat(t)[:, 0:1024].rearrange("p (m x) -> p m x", m=MT) for t in (k.vs, k.vw)]
        kT = [sb(f"cacheT{j}", [P, 1536]) for j in range(2)]
        Qz, Qf = sb("Qz", [P, DB, P]), sb("Qf", [P, 2, P])
        Qm = sb("Qm", [P, DB, 2, P])
        Pr = sb("Pr", [P, CM + NCMP])
        PTs = k.qT[:, :, 0:512]
        imp = sb("imp", [P, 72])
        sel, pen = sb("sel", [P, 2, 16]), sb("pen", [P, 16])
        nm, den, rs = sb("nm_s", [P, 3, 3]), sb("den_s", [P, 3, 3]), sb("rs_s", [P, 3, 3])
        gr, gm = sb("gate_rows", [P, 2, 3]), sb("gate_all", [P, 24])
        sS, sW, sN = ps("sS", [P, 1024]), ps("sW", [P, 512]), ps("sN", [P, 512])
        tp = [ps(f"stp{j}", [P, 4, P]) for j in range(3)]
        ob = ps("sob", [P, 512])
        s_z, s_q = sem("queries_zeroed"), sem("queries_spread")
        s_t, s_te = sem("cache_transposed"), [sem("cacheT_evicted_dve"), sem("cacheT_evicted_act")]
        s_kb, s_n, s_g, s_gr = sem("row_scored"), sem("new_and_cmp_scored"), sem("gates_spread"), sem("gate_rows_ready")
        s_nm, s_ex, s_hp, s_h = sem("s_neg_max"), sem("s_exp_done"), sem("cmp_normed"), sem("heads_summed")
        s_p, s_pt, s_pe, s_pv, s_mix = (sem("s_p_scaled"), sem("s_p_transposed"), sem("s_pT_evicted"), sem("s_values_done"),
                                        sem("s_mix_written"))
        s_sb = sem("s_scores_read")
        s_dc = sem("sample_dve_chain")
        done_by = lambda n, e: (n + 1 - e) // 2
        NTR = [3, 3, 1]
        rows_of = [range(0, 4), range(4, 8), range(0, 8)]
        g0 = [0, 12, 24, 32]
        b0 = [0, 4, 8, 16]
        block = ctx.enter_context(nc.Block())

        @block.sync
        def _(sp):
            mem = i["cache_mem_kv"][0].rearrange("b (m p) k h d -> p b m (k h d)", p=P)
            for b in range(DB):
                sp.dma_start(nat_m[b], mem[:, b]).then_inc(s_x[2], 16)
            sp.wait_ge(s_pv, 1)
            load_caches(sp, k, 1, False)
            sp.wait_ge(s_pv, 2)
            load_w_out(sp, k)

        @block.tensor
        def _(pe):
            ident = C[:, at["ident"]]

            def turn(st, r):
                for j in range(NTR[st]):
                    n = g0[st] + r * NTR[st] + j
                    if n >= 3:
                        for e in range(2):
                            pe.wait_ge(s_te[e], done_by(n - 2, e))
                    for m in range(4):
                        if st == 2:
                            src = nat_m[r][:, m % 2, (m // 2) * P:(m // 2 + 1) * P]
                        else:
                            src = nat[:, r, 4 * j + m, 0:P] if j < 2 else natw[:, r, m, 0:P]
                        mm = nc.tensor.transpose(tp[n % 3][:, m, :], src, ident)
                    mm.then_inc(s_t, 1)

            def score(st, r):
                n = g0[st] + (r + 1) * NTR[st]
                for e in range(2):
                    pe.wait_ge(s_te[e], done_by(n, e))
                t = kT[r % 2]
                first, last = r == 0, r == len(rows_of[st]) - 1
                if first and st:
                    pe.wait_ge(s_sb, st)
                if st == 2:
                    for m in range(2):
                        mm = nc.tensor.matmul(sS[:, 0:256], Qm[:, r, m, :], t[:, m * 256:m * 256 + 256],
                                              start=first and m == 0, stop=last and m == 1)
                else:
                    q = Qz[:, NB * st + r, :]
                    for m in range(2):
                        nc.tensor.matmul(sS[:, m * 512:m * 512 + 512], q, t[:, m * 512:m * 512 + 512], start=first, stop=last)
                    mm = nc.tensor.matmul(sW[:], q, t[:, 1024:1536], start=first, stop=last)
                mm.then_inc(s_kb, 1)

            pe.wait_ge(s_q, 1)
            for st in range(3):
                if st < 2:
                    if st:
                        pe.wait_ge(s_sb, st)
                    for b in range(NB):
                        nc.tensor.matmul(sN[:, 64:64 + NCMP], Qz[:, NB * st + b, :], k.kcT[:, NB * st + b, :],
                                         start=(b == 0), stop=(b == NB - 1))
                    nc.tensor.matmul(sN[:, 0:SR], Qf[:, st, :], k.ksT[:, S:T], start=True, stop=True)
                    nc.tensor.matmul(sN[:, SR:2 * SR], Qf[:, st, :], k.kwT[:, S:T], start=True, stop=True)
                    nc.tensor.matmul(sN[:, 128:152], B[:SR, at["rowsel"]][:, st * P:st * P + P], k.gate[:SR, PT, :],
                                     start=True, stop=True).then_inc(s_n, 1)
                    pe.wait_ge(s_hp, st + 1)
                    nc.tensor.matmul(sN[:, 192:192 + NCMP], B[:, at["headsum"]], Pr[:, CM:], start=True, stop=True).then_inc(s_h, 1)
                npool = NB * len(POOL_PAGES)
                pe.wait_ge(s_x[st], 16 * (8 if st == 2 else NB * (PAGES + 1) - npool))
                if st < 2:
                    pe.wait_ge(k.s_cache_pool[st], 16 * npool)
                R = rows_of[st]
                turn(st, 0)
                for r in range(len(R)):
                    if r + 1 < len(R):
                        turn(st, r + 1)
                    score(st, r)
                pe.wait_ge(s_p, st + 1)
                n = g0[3]
                for e in range(2):
                    pe.wait_ge(s_te[e], done_by(g0[st + 1], e))
                if st < 2:
                    for j in range(3):
                        c0 = (SL, SL + 512, WN)[j]
                        for m in range(4):
                            mm = nc.tensor.transpose(tp[j][:, m, :], Pr[:, c0 + m * P:c0 + m * P + P], ident)
                        mm.then_inc(s_pt, 1)
                    pe.wait_ge(s_pe, 4 * st + 1)
                    nc.tensor.transpose(tp[0][:SR, 0, :], Pr[:, NS:NS + SR], ident)
                    nc.tensor.transpose(tp[0][:SR, 1, :], Pr[:, NW:NW + SR], ident)
                    nc.tensor.transpose(tp[0][:NCMP, 2, :], Pr[:, CM:], ident).then_inc(s_pt, 1)
                    pe.wait_ge(s_pe, 4 * st + 4)
                    if st:
                        pe.wait_ge(s_mix, st)
                    for b in range(NB):
                        c = slice(b * 32, b * 32 + 32)
                        out = ob[:, c]
                        pT = lambda j, m, w=P: PTs[:w, j, m * P + b * 32:m * P + b * 32 + 32]
                        for pg in range(PAGES):
                            nc.tensor.matmul(out, nat[:, b, pg, P:2 * P], pT(pg // 4, pg % 4), start=(pg == 0), stop=False)
                        for m in range(4):
                            nc.tensor.matmul(out, natw[:, b, m, P:2 * P], pT(2, m), start=False, stop=False)
                        nc.tensor.matmul(out, k.vs[:SR, PT, :], pT(3, 0, SR), start=False, stop=False)
                        nc.tensor.matmul(out, k.vw[:SR, PT, :], pT(3, 1, SR), start=False, stop=False)
                        mm = nc.tensor.matmul(out, k.vc[:, NB * st + b, :], pT(3, 2, NCMP), start=False, stop=True)
                    mm.then_inc(s_pv, 1)
                else:
                    for m in range(2):
                        mm = nc.tensor.transpose(tp[0][:, m, :], Pr[:, m * P:m * P + P], ident)
                    mm.then_inc(s_pt, 1)
                    pe.wait_ge(s_pe, 9)
                    pe.wait_ge(s_mix, 2)
                    for b in range(DB):
                        for h in range(2):
                            for m in range(2):
                                mm = nc.tensor.matmul(ob[:, h * P + b * 16:h * P + b * 16 + 16], nat_m[b][:, m, 256 + h * P:384 + h * P],
                                                      PTs[:, 0, m * P + b * 16:m * P + b * 16 + 16], start=(m == 0), stop=(m == 1))
                    mm.then_inc(s_pv, 1)

        def evict_keys(eng, copy, st, r, e):
            for j in range(NTR[st]):
                n = g0[st] + r * NTR[st] + j
                if n % 2 != e:
                    continue
                eng.wait_ge(s_t, n + 1)
                if b0[st] + r >= 2:
                    eng.wait_ge(s_kb, max(b0[st] + r - 1, b0[st]) if r < 2 else b0[st] + r - 1)
                copy(kT[r % 2][:, 512 * j:512 * j + 512], tp[n % 3][:].rearrange("p a b -> p (a b)")).then_inc(s_te[e], 1)

        @block.scalar
        def _(act):
            for st in range(3):
                nr = len(rows_of[st])
                if st < 2:
                    act.wait_ge(s_nm, (1 if st == 0 else 4))
                    nc.scalar.activation(Pr[:, CM:], sN[:, 64:64 + NCMP], ACT.Exp, bias=nm[:, st, 0:1], accum_out=den[:, st, 0:1]).then_inc(s_ex, 1)
                for r in range(nr):
                    evict_keys(act, nc.scalar.copy, st, r, 1)
                if st < 2:
                    for j, (a, b) in enumerate(((SL, WN), (WN, CM))):
                        act.wait_ge(s_nm, 3 * st + 2 + j)
                        nc.scalar.activation(Pr[:, a:b], Pr[:, a:b], ACT.Exp, bias=nm[:, st, 1 + j:2 + j],
                                             accum_out=den[:, st, 1 + j:2 + j]).then_inc(s_ex, 1)
                else:
                    act.wait_ge(s_nm, 7)
                    nc.scalar.activation(Pr[:, 0:256], sS[:, 0:256], ACT.Exp, bias=nm[:, 2, 0:1], accum_out=den[:, 2, 0:1]).then_inc(s_ex, 1)

        @block.gpsimd
        def _(pool):
            nc.gpsimd.memset(Qz[:], 0.0)
            nc.gpsimd.memset(Qf[:], 0.0)
            nc.gpsimd.memset(Qm[:], 0.0).then_inc(s_z, 1)
            pool.wait_ge(s_pv, 1)
            load_caches(pool, k, 1, True)

        @block.vector
        def _(dve):
            n_dc = [0]

            def link(ins):
                n_dc[0] += 1
                ins.then_inc(s_dc, 1)
                dve.wait_ge(s_dc, n_dc[0])

            nc.vector.memset(imp[:], 0.0)
            nc.vector.memset(pen[:], 0.0)
            dve.wait_ge(s_z, 1)
            for st in range(2):
                for g in range(G):
                    h = slice(64 * g, 64 * g + 64)
                    src = k.qT[h, :, S + 16 * st:S + 16 * st + 16].rearrange("p c (b q) -> p b c q", q=QS)
                    for b in range(NB):
                        c0 = b * 32 + g * 16
                        nc.vector.tensor_copy(Qz[h, NB * st + b, c0:c0 + 16].rearrange("p (c q) -> p c q", q=QS), src[:, b])
                        nc.vector.tensor_copy(Qf[h, st, c0:c0 + 16].rearrange("p (c q) -> p c q", q=QS), src[:, b])
            for b in range(DB):
                for a in range(2):
                    h = slice(64 * a, 64 * a + 64)
                    for m in range(2):
                        c0 = b * 16 + (2 * m + a) * QS
                        last = nc.vector.tensor_copy(Qm[h, b, m, c0:c0 + QS], k.mqT[h, m, S + b * QS:S + (b + 1) * QS])
            last.then_inc(s_q, 1)
            mx = lambda out, src: nc.vector.tensor_reduce(out, src, AX.X, ALU.max, negate=True)
            for st in range(3):
                if st < 2:
                    dve.wait_ge(s_n, st + 1)
                    mx(nm[:, st, 0:1], sN[:, 64:64 + NCMP])
                    link(nc.vector.tensor_tensor(gm[:].rearrange("p (h x) -> p h x", x=3), sN[:, 128:152].rearrange("p (h x) -> p h x", x=3),
                                                 bc(B[:, at["rowhead"]], 3), ALU.mult))
                    if st:
                        dve.wait_ge(s_pt, 4)
                    nc.vector.tensor_reduce(gr[:, st, :], gm[:].rearrange("p (h x) -> p x h", x=3), AX.X, ALU.add).then_inc(s_nm, 1)
                    dve.wait_ge(s_ex, 3 * st + 1)
                    link(nc.vector.reciprocal(rs[:, st, 0:1], den[:, st, 0:1]))
                    nc.vector.tensor_scalar(Pr[:, CM:], Pr[:, CM:], rs[:, st, 0:1], None, ALU.mult).then_inc(s_hp, 1)
                    dve.wait_ge(s_h, st + 1)
                    link(nc.vector.tensor_copy(imp[:, 1:1 + NCMP], sN[:, 192:192 + NCMP]))
                    ps14, eq = sel[:, 0, 0:14], sel[:, 1, 0:14]
                    link(nc.vector.tensor_reduce(ps14, imp[:, 4:60].rearrange("p (j r) -> p j r", r=4), AX.X, ALU.add))
                    link(nc.vector.tensor_tensor(ps14, ps14, imp[:, 8:64].rearrange("p (j r) -> p j r", r=4)[:, :, 0], ALU.add))
                    link(nc.vector.tensor_reduce(sel[:, 0, 14:15], ps14, AX.X, ALU.min))
                    link(nc.vector.tensor_scalar(eq, ps14, sel[:, 0, 14:15], None, ALU.is_equal))
                    link(nc.vector.tensor_tensor(eq, eq, B[:, at["blockidx"]], ALU.mult))
                    link(nc.vector.tensor_reduce(sel[:, 1, 14:15], eq, AX.X, ALU.max))
                    link(nc.vector.tensor_scalar(pen[:, 1:15], B[:, at["blockidx"]], sel[:, 1, 14:15], NEG, ALU.is_equal, ALU.mult))
                for r in range(len(rows_of[st])):
                    evict_keys(dve, nc.vector.tensor_copy, st, r, 0)
                dve.wait_ge(s_kb, b0[st + 1])
                if st < 2:
                    nmk = B[:, at["newmask"]][:, st * SR:(st + 1) * SR]
                    nc.vector.tensor_tensor(Pr[:, SL:NS].rearrange("p (j x) -> p j x", x=64), sS[:].rearrange("p (j x) -> p j x", x=64),
                                            bc(pen[:], 64), ALU.add)
                    link(nc.vector.tensor_tensor(Pr[:, NS:WN], sN[:, 0:SR], nmk, ALU.add))
                    mx(nm[:, st, 1:2], Pr[:, SL:WN]).then_inc(s_nm, 1)
                    nc.vector.tensor_tensor(Pr[:, WN:NW], sW[:], B[:, at["oldwin"]], ALU.add)
                    link(nc.vector.tensor_tensor(Pr[:, NW:CM], sN[:, SR:2 * SR], nmk, ALU.add))
                    mx(nm[:, st, 2:3], Pr[:, WN:CM]).then_inc(s_nm, 1)
                    nc.vector.tensor_scalar(rs[:, st, 0:1], gr[:, st, 0:1], 1.0, None, ALU.mult).then_inc(s_sb, 1)
                    dve.wait_ge(s_ex, 3 * st + 3)
                    link(nc.vector.reciprocal(rs[:, st, 1:3], den[:, st, 1:3]))
                    nc.vector.tensor_scalar(Pr[:, SL:WN], Pr[:, SL:WN], rs[:, st, 1:2], gr[:, st, 1:2], ALU.mult, ALU.mult)
                    nc.vector.tensor_scalar(Pr[:, WN:CM], Pr[:, WN:CM], rs[:, st, 2:3], gr[:, st, 2:3], ALU.mult, ALU.mult)
                    nc.vector.tensor_scalar(Pr[:, CM:], Pr[:, CM:], gr[:, st, 0:1], None, ALU.mult).then_inc(s_p, 1)
                    for j in range(3):
                        dve.wait_ge(s_pt, 4 * st + j + 1)
                        if st and j == 0:
                            dve.wait_ge(s_pv, st)
                        nc.vector.tensor_copy(PTs[:, j, :], tp[j][:].rearrange("p a b -> p (a b)")).then_inc(s_pe, 1)
                    dve.wait_ge(s_pt, 4 * st + 4)
                    nc.vector.tensor_copy(PTs[:SR, 3, 0:2 * P], tp[0][:SR, 0:2, :].rearrange("p a b -> p (a b)"))
                    nc.vector.tensor_copy(PTs[:NCMP, 3, 2 * P:3 * P], tp[0][:NCMP, 2, :]).then_inc(s_pe, 1)
                    dve.wait_ge(s_pv, st + 1)
                    for g in range(G):
                        h = slice(64 * g, 64 * g + 64)
                        for b in range(NB):
                            c0, t0 = b * 32 + g * 16, S + (NB * st + b) * QS
                            last = nc.vector.tensor_copy(k.mixT[h, 0:4, t0:t0 + QS], ob[h, c0:c0 + 16].rearrange("p (c q) -> p c q", q=QS))
                    last.then_inc(s_mix, 1)
                else:
                    mx(nm[:, 2, 0:1], sS[:, 0:256]).then_inc(s_nm, 1)
                    dve.wait_ge(s_ex, 7)
                    link(nc.vector.reciprocal(rs[:, 2, 0:1], den[:, 2, 0:1]))
                    nc.vector.tensor_scalar(Pr[:, 0:256], Pr[:, 0:256], rs[:, 2, 0:1], None, ALU.mult).then_inc(s_p, 1)
                    dve.wait_ge(s_pt, 9)
                    nc.vector.tensor_copy(PTs[:, 0, 0:2 * P], tp[0][:, 0:2, :].rearrange("p a b -> p (a b)")).then_inc(s_pe, 1)
                    dve.wait_ge(s_pv, 3)
                    for a in range(2):
                        h = slice(64 * a, 64 * a + 64)
                        for m in range(2):
                            src = ob[h, m * P:m * P + P].rearrange("p (b h q) -> p b h q", h=4, q=QS)[:, :, 2 * m + a, :]
                            nc.vector.tensor_copy(k.mixT[h, 6 + m, S:T].rearrange("p (b q) -> p b q", q=QS), src)


def phase_retention_out(nc, k):
    i, o, at, C, B = k.i, k.o, k.at, k.C, k.B
    with ExitStack() as ctx:
        sb = lambda n, s, d=F32: ctx.enter_context(nc.sbuf_tensor(n, s, d))
        ps = lambda n, s, d=F32: ctx.enter_context(nc.psum_tensor(n, s, d))
        sem = k.sem
        st = sb("state", [P, 2, DB, HD])
        qx, vz, sTm = sb("qxi_z", [P, 2, DB, SR]), sb("v_z", [SR, 4, DB, HD]), sb("sTm_s", [SR, 4, SR])
        sq, sg, gain = sb("ret_sq", [P, NT, 256]), sb("ret_sig", [P, NT, 256]), sb("ret_gain", [P, HD])
        ms = sb("ret_ms", [P, NT * 4])
        sT = [ps(f"rsT{a}", [SR, 2, SR]) for a in range(2)]
        op = [ps(f"rso{a}", [SR, 2, HD]) for a in range(2)]
        dR = [ps(f"rdR{a}", [P, 512]) for a in range(2)]
        tp = [ps(f"rtp{a}", [P, 4, P]) for a in range(2)]
        s_l, s_z, s_q, s_s, s_m, s_o, s_d = (sem("state_loaded"), sem("qxi_zeroed"), sem("qxi_spread"), sem("s_ret_scores"),
                                             sem("s_ret_masked"), sem("s_ret_out"), sem("s_ret_delta"))
        s_sg, s_ms, s_rt, s_f, s_t, s_dc = (sem("silu_sigmoid"), sem("ret_mean_square"), sem("ret_root"), sem("ret_final"),
                                            sem("ret_transposed"), sem("ret_dve_chain"))
        s_e, s_st, s_out = sem("ret_evicted"), sem("state_updated"), sem("state_stored")
        block = ctx.enter_context(nc.Block())
        dram_state = lambda ap: ap[0].rearrange("b (i a) d e -> (a d) i b e", a=2)

        @block.sync
        def _(sp):
            for m in range(2):
                sp.dma_start(st[:, m], dram_state(i["state_ret"])[:, m]).then_inc(s_l, 16)
            sp.dma_start(gain[:], i["ret_norm_g"].broadcast_to([P, HD])).then_inc(s_l, 16)
            load_caches(sp, k, 0, False)
            sp.wait_ge(s_st, 1)
            for m in range(2):
                sp.dma_start(dram_state(o["ret_s"])[:, m], st[:, m]).then_inc(s_out, 16)
            sp.wait_ge(s_out, 32)

        @block.gpsimd
        def _(pool):
            nc.gpsimd.memset(qx[:], 0.0).then_inc(s_z, 1)
            load_caches(pool, k, 0, True)

        @block.tensor
        def _(pe):
            for h in range(4):
                b = 64 * (h % 2)
                mm = nc.tensor.matmul(sT[h % 2][:, h // 2, :], k.rT[b:b + 64, 4 + h // 2, :SR], k.rT[b:b + 64, h // 2, :SR],
                                      start=True, stop=True)
            mm.then_inc(s_s, 1)
            pe.wait_ge(s_l, 48)
            pe.wait_ge(s_q, 1)
            pe.wait_ge(s_m, 1)
            for h in range(4):
                b = 64 * (h % 2)
                out = op[h % 2][:, h // 2, :]
                nc.tensor.matmul(out, sTm[:, h, :], k.rvs[:, h * 64:h * 64 + 64], start=True, stop=False)
                for r in range(DB):
                    mm = nc.tensor.matmul(out, qx[b:b + 64, h // 2, r, :], st[b:b + 64, h // 2, r, :], start=False, stop=(r == DB - 1))
            mm.then_inc(s_o, 1)
            for h in range(4):
                b = 64 * (h % 2)
                mm = nc.tensor.matmul(dR[h // 2][b:b + 64, :], k.kz[:SR, h * 64:h * 64 + 64], vz[:, h].rearrange("p b e -> p (b e)"),
                                      start=True, stop=True)
            mm.then_inc(s_d, 1)
            pe.wait_ge(s_f, 1)
            for t in range(NT):
                R = rows(t)
                if t >= 2:
                    pe.wait_ge(s_e, t - 1)
                for m in range(2):
                    mm = nc.tensor.transpose(tp[t % 2][:, m, :R], k.oret[:R, t, m * P:m * P + P], C[:R, at["ident"]][:, :R])
                mm.then_inc(s_t, 1)

        @block.scalar
        def _(act):
            for R, ts in ((P, slice(0, PT)), (SR, slice(PT, NT))):
                nc.scalar.activation(sg[:R, ts], k.rg[:R, ts], ACT.Sigmoid).then_inc(s_sg, 1)
            act.wait_ge(s_ms, 2)
            nc.scalar.activation(ms[:, 0:4 * PT], ms[:, 0:4 * PT], ACT.Sqrt)
            nc.scalar.activation(ms[:SR, 4 * PT:], ms[:SR, 4 * PT:], ACT.Sqrt).then_inc(s_rt, 1)
            for t in range(NT):
                act.wait_ge(s_t, t + 1)
                nc.scalar.copy(k.mixT[:, 4:6, t * P:t * P + rows(t)], tp[t % 2][:, 0:2, :rows(t)]).then_inc(s_e, 1)

        @block.vector
        def _(dve):
            n_dc = [0]

            def link(ins):
                n_dc[0] += 1
                ins.then_inc(s_dc, 1)
                dve.wait_ge(s_dc, n_dc[0])

            dve.wait_ge(s_z, 1)
            for r in range(DB):
                nc.vector.tensor_copy(qx[:, :, r, r * QS:(r + 1) * QS], k.rT[:, 2:4, r * QS:(r + 1) * QS])
            for h in range(4):
                last = nc.vector.tensor_tensor(vz[:, h], k.rvs[:, h * 64:h * 64 + 64].unsqueeze(1).broadcast_to([SR, DB, HD]),
                                               bc(B[:SR, at["ofrow"]], HD), ALU.mult)
            last.then_inc(s_q, 1)
            dve.wait_ge(s_s, 1)
            dm = B[:SR, at["dmaskTs"]].rearrange("p (i a n) -> p a i n", a=2, i=2)
            so = sTm[:].rearrange("p (i a) n -> p a i n", a=2)
            nc.vector.tensor_tensor(so[:, 0], sT[0][:], dm[:, 0], ALU.mult)
            nc.vector.tensor_tensor(so[:, 1], sT[1][:], dm[:, 1], ALU.mult).then_inc(s_m, 1)
            dve.wait_ge(s_o, 1)
            for a in range(2):
                last = nc.vector.tensor_copy(k.oret[:SR, PT, :].rearrange("p (i a e) -> p a i e", i=2, a=2)[:, a], op[a][:])
            link(last)
            dve.wait_ge(s_d, 1)
            for m in range(2):
                f = st[:, m].rearrange("p b e -> p (b e)")
                last = nc.vector.scalar_tensor_tensor(out=f, in0=f, scalar=C[:, at["decay"]][:, 2 + m:3 + m], in1=dR[m][:],
                                                      op0=ALU.mult, op1=ALU.add)
            last.then_inc(s_st, 1)
            parts = ((P, slice(0, PT), 0, 4 * PT), (SR, slice(PT, NT), 4 * PT, 4 * NT))
            for R, ts, a, b in parts:
                link(nc.vector.tensor_tensor(sq[:R, ts], k.oret[:R, ts], k.oret[:R, ts], ALU.mult))
                link(nc.vector.tensor_reduce(ms[:R, a:b], sq[:R, ts].rearrange("p t (h d) -> p (t h) d", d=64), AX.X, ALU.add))
                nc.vector.tensor_scalar(ms[:R, a:b], ms[:R, a:b], 1.0 / HD, EPS, ALU.mult, ALU.add).then_inc(s_ms, 1)
            dve.wait_ge(s_sg, 2)
            for R, ts, a, b in parts:
                hv = lambda x: x[:R, ts].rearrange("p t (h d) -> p (t h) d", d=64)
                link(nc.vector.tensor_tensor(sg[:R, ts], sg[:R, ts], k.rg[:R, ts], ALU.mult))
                link(nc.vector.tensor_tensor(hv(sg), hv(sg), gain[:R].unsqueeze(1).broadcast_to([R, b - a, HD]), ALU.mult))
            dve.wait_ge(s_rt, 1)
            for R, ts, a, b in parts:
                hv = lambda x: x[:R, ts].rearrange("p t (h d) -> p (t h) d", d=64)
                link(nc.vector.reciprocal(ms[:R, a:b], ms[:R, a:b]))
                link(nc.vector.tensor_tensor(hv(k.oret), hv(k.oret), bc(ms[:R, a:b], HD), ALU.mult))
                last = nc.vector.tensor_tensor(k.oret[:R, ts], k.oret[:R, ts], sg[:R, ts], ALU.mult)
            last.then_inc(s_f, 1)


def phase_out(nc, k):
    i, at, C = k.i, k.at, k.C
    with ExitStack() as ctx:
        sb = lambda n, s, d=F32: ctx.enter_context(nc.sbuf_tensor(n, s, d))
        ps = lambda n, s, d=F32: ctx.enter_context(nc.psum_tensor(n, s, d))
        sem = k.sem
        w = k.w_out
        wr = sb("w_router", [P, KC, NE])
        g2, br = k.qT[:, 0, 0:D], k.qT[:, 1, 0:NE]
        zero = k.qT[0:1, 2, 0:D]
        x = [sb(f"xr{j}", [P, D]) for j in range(2)]
        x2 = [sb(f"x2_{j}", [P, D]) for j in range(2)]
        h = [sb(f"h{j}", [P, D]) for j in range(2)]
        hT = sb("hT_e", [P, KC, P])
        ss = sb("ss_e", [P, 4 * NT])
        op = [[ps(f"eo{j}{n}", [P, 512]) for n in range(2)] for j in range(2)]
        tp = [ps(f"etp{j}", [P, 4, P]) for j in range(2)]
        rp = ps("erp", [P, NE])
        s_w, s_g, s_x = k.s_w_out, sem("e_small_loaded"), [sem(f"xr_loaded{j}") for j in range(2)]
        s_o, s_x2, s_ss, s_ms, s_rt, s_h = (sem("e_projected"), sem("x2_ready"), sem("e_squares"), sem("e_mean_square"),
                                            sem("e_root"), sem("h_ready"))
        s_t, s_te, s_r, s_l, s_z = sem("h_transposed"), sem("e_hT_ready"), sem("e_routed"), sem("logits_ready"), sem("zero_row")
        s_st = [sem(f"x2_h_stored{j}") for j in range(2)]
        s_dc, s_zo = sem("e_dve_chain"), sem("zero_row_stored")
        xsrc = lambda t: i["x_prompt"][0, t * P:(t + 1) * P, :] if t < PT else i["x_sample"].rearrange("b s d -> (b s) d")
        block = ctx.enter_context(nc.Block())

        @block.sync
        def _(sp):
            def load_x(t):
                if t >= 2:
                    sp.wait_ge(s_x2, t - 1)
                sp.dma_start(x[t % 2][:rows(t), :], xsrc(t)).then_inc(s_x[t % 2], 16)

            load_x(0)
            load_x(1)
            sp.dma_start(g2, i["norm2_g"].broadcast_to([P, D])).then_inc(s_g, 16)
            sp.dma_start(br, i["b_router"].broadcast_to([P, NE])).then_inc(s_g, 16)
            sp.dma_start(wr[:], i["w_router"][0].rearrange("(c p) n -> p c n", p=P)).then_inc(s_g, 16)
            sp.wait_ge(s_z, 1)
            sp.dma_start(k.h_dram[T:T + 1, :], zero).then_inc(s_zo, 16)
            for t in range(NT):
                if t + 2 < NT:
                    load_x(t + 2)
                sp.wait_ge(s_h, t + 1)
                R = rows(t)
                sp.dma_start(k.x2_dram[t * P:t * P + R, :], x2[t % 2][:R, :]).then_inc(s_st[t % 2], 16)
                sp.dma_start(k.h_dram[t * P:t * P + R, :], h[t % 2][:R, :]).then_inc(s_st[t % 2], 16)
            sp.wait_ge(s_zo, 16)
            sp.wait_ge(s_st[0], 32 * 5)
            sp.wait_ge(s_st[1], 32 * 4)

        @block.tensor
        def _(pe):
            def router(t):
                R = rows(t)
                pe.wait_ge(s_h, t + 1)
                for j in range(2):
                    if t >= 1:
                        pe.wait_ge(s_te, 2 * t - 1 + j)
                    for m in range(4):
                        c = 4 * j + m
                        mm = nc.tensor.transpose(tp[j][:, m, :R], h[t % 2][:R, c * P:c * P + P], C[:R, at["ident"]][:, :R])
                    mm.then_inc(s_t, 1)
                pe.wait_ge(s_te, 2 * t + 2)
                if t >= 1:
                    pe.wait_ge(s_l, t)
                for c in range(KC):
                    mm = nc.tensor.matmul(rp[:R, :], hT[:, c, :R], wr[:, c, :], start=(c == 0), stop=(c == KC - 1))
                mm.then_inc(s_r, 1)

            for t in range(NT):
                R = rows(t)
                if t >= 2:
                    pe.wait_ge(s_x2, t - 1)
                for n in range(2):
                    if t == 0:
                        pe.wait_ge(s_w[n], 16 * 9)
                    for c in range(KC):
                        mm = nc.tensor.matmul(op[t % 2][n][:R, :], k.mixT[:, c, t * P:t * P + R], w[:, c, n * 512:n * 512 + 512],
                                              start=(c == 0), stop=(c == KC - 1))
                mm.then_inc(s_o, 1)
                if t == 0:
                    pe.wait_ge(s_g, 48)
                else:
                    router(t - 1)
            router(NT - 1)

        @block.scalar
        def _(act):
            def evict(t):
                R = rows(t)
                for j in range(2):
                    act.wait_ge(s_t, 2 * t + 1 + j)
                    if t >= 1 and j == 0:
                        act.wait_ge(s_r, t)
                    nc.scalar.copy(hT[:, 4 * j:4 * j + 4, :R], tp[j][:, :, :R]).then_inc(s_te, 1)

            for t in range(NT):
                R = rows(t)
                act.wait_ge(s_x2, t + 1)
                if t >= 2:
                    act.wait_ge(s_st[t % 2], 32 * (t // 2))
                nc.scalar.activation(h[t % 2][:R, :], x2[t % 2][:R, :], ACT.Square, accum_out=ss[:R, t:t + 1]).then_inc(s_ss, 1)
                act.wait_ge(s_ms, t + 1)
                nc.scalar.activation(ss[:R, 2 * NT + t:2 * NT + t + 1], ss[:R, NT + t:NT + t + 1], ACT.Sqrt).then_inc(s_rt, 1)
                evict(t)

        @block.vector
        def _(dve):
            n_dc = [0]

            def link(ins):
                n_dc[0] += 1
                ins.then_inc(s_dc, 1)
                dve.wait_ge(s_dc, n_dc[0])

            nc.vector.memset(zero, 0.0).then_inc(s_z, 1)
            nc.vector.memset(k.logits[:], 0.0)
            for t in range(NT):
                R, xx, hh = rows(t), x2[t % 2], h[t % 2]
                dve.wait_ge(s_o, t + 1)
                dve.wait_ge(s_x[t % 2], 16 * (t // 2 + 1))
                if t >= 2:
                    dve.wait_ge(s_st[t % 2], 32 * (t // 2))
                for n in range(2):
                    c = slice(n * 512, n * 512 + 512)
                    last = nc.vector.tensor_tensor(xx[:R, c], op[t % 2][n][:R, :], x[t % 2][:R, c], ALU.add)
                last.then_inc(s_x2, 1)
                dve.wait_ge(s_ss, t + 1)
                nc.vector.tensor_scalar(ss[:R, NT + t:NT + t + 1], ss[:R, t:t + 1], 1.0 / D, EPS, ALU.mult, ALU.add).then_inc(s_ms, 1)
                dve.wait_ge(s_rt, t + 1)
                link(nc.vector.reciprocal(ss[:R, 3 * NT + t:3 * NT + t + 1], ss[:R, 2 * NT + t:2 * NT + t + 1]))
                if t == 0:
                    dve.wait_ge(s_g, 48)
                nc.vector.scalar_tensor_tensor(out=hh[:R, :], in0=xx[:R, :], scalar=ss[:R, 3 * NT + t:3 * NT + t + 1], in1=g2[:R],
                                               op0=ALU.mult, op1=ALU.mult).then_inc(s_h, 1)
                if t >= 1:
                    dve.wait_ge(s_r, t)
                    nc.vector.tensor_tensor(k.logits[:rows(t - 1), t - 1, :], rp[:rows(t - 1), :], br[:rows(t - 1)], ALU.add).then_inc(s_l, 1)
            dve.wait_ge(s_r, NT)
            nc.vector.tensor_tensor(k.logits[:SR, PT, :], rp[:SR, :], br[:SR], ALU.add).then_inc(s_l, 1)


def load_piece(sp, k, e, j):
    if j < 4:
        wu = k.i["w_up"][0].rearrange("e (k p) (h n) -> e p k h n", p=P, h=2)
        for h in range(2):
            sp.dma_start(k.W[j][:, :, h * 256:h * 256 + 256],
                         wu[bass.ds(e, 1), :, :, h, j * 256:j * 256 + 256].rearrange("o p k n -> (o p) k n")).then_inc(k.s_w[j], 16)
    else:
        wd = k.i["w_down"][0].rearrange("e (k p) n -> e p k n", p=P)
        j4 = j - 4
        sp.dma_start(k.W[j][:], wd[bass.ds(e, 1), :, :, j4 * 512:j4 * 512 + 512].rearrange("o p k n -> (o p) k n")).then_inc(k.s_w[j], 16)


def phase_route(nc, k):
    i, at, C, B = k.i, k.at, k.C, k.B
    BASE = CAP * NE
    with ExitStack() as ctx:
        sb = lambda n, s, d=F32: ctx.enter_context(nc.sbuf_tensor(n, s, d))
        ps = lambda n, s, d=F32: ctx.enter_context(nc.psum_tensor(n, s, d))
        sem = k.sem
        hot = sb("onehot", [P, TOPK, NT, NE])
        t1, M, slot, alt = sb("rt1", [P, NT, NE]), sb("chosen", [P, NT, NE]), sb("slot", [P, NT, NE]), sb("alt", [P, NT, NE])
        e64, tv, ti = sb("e64", [P, NE]), sb("topv", [P, TOPK, NT]), sb("topi", [P, NT])
        gs = sb("gsum", [P, NT])
        ones = sb("ones_r", [P, P])
        cnt, nb, inc, st = sb("cnt", [P, NE]), sb("nb", [P, NE]), sb("inc", [P, NE]), sb("start", [P, NE])
        ob = sb("obt", [P, NOB, NE])
        obf = sb("obf", [P, NOB])
        df = sb("destf", [P, TOPK, NT])
        fill = sb("fill", [P, NSLOT // P], I32)
        braw = sb("bias_rows", [P, 6, P])
        rk, ct = ps("rankp", [P, NT * NE]), ps("countp", [P, NE])
        bt = [ps(f"biasp{j}", [P, 4, P]) for j in range(2)]
        s_m, s_rk, s_dc, s_d, s_f, s_ini, s_sc, s_ix = (sem("chosen_ready"), sem("ranks_done"), sem("route_dve_chain"), sem("dest_ready"),
                                                  sem("fill_ready"), sem("slots_filled"), sem("tokens_scattered"), sem("idx_loaded"))
        s_tb = sem("route_tables_loaded")
        s_e, s_ge, s_b, s_bt = sem("gate_diff"), sem("gate_exp"), sem("bias_loaded"), sem("bias_transposed")
        block = ctx.enter_context(nc.Block())
        table = k.slot_dram

        @block.sync
        def _(sp):
            bu = i["b_up"][0].rearrange("e (c p) -> (e c) p", p=P).rearrange("(t r) p -> r t p", r=P)
            bd = i["b_down"][0].rearrange("e (c p) -> (e c) p", p=P).rearrange("(t r) p -> r t p", r=P)
            sp.dma_start(B[:], i["tables_b"]).then_inc(s_tb, 16)
            sp.dma_start(braw[:, 0:4, :], bu).then_inc(s_b, 16)
            sp.dma_start(braw[:, 4:6, :], bd).then_inc(s_b, 16)
            for j in range(6):
                load_piece(sp, k, 0, j)
            sp.wait_ge(s_f, 1)
            sp.dma_start(table.rearrange("(p s) o -> p (s o)", p=P), fill[:]).then_inc(s_ini, 16)
            sp.wait_ge(s_sc, 16 * TOPK * NT)
            base = table[0:BASE, :].rearrange("(r e) o -> r (e o)", e=NE)
            sp.dma_start(k.idxA[:], base[0:P, :]).then_inc(s_ix, 16)
            sp.dma_start(k.idxB[:], base[P:CAP, :]).then_inc(s_ix, 16)
            with nc.allow_non_contiguous_dma(reason="slots of the overflow blocks, one number each"):
                sp.dma_start(k.idxO[:], table[BASE:NSLOT, :].rearrange("(b p) o -> p (b o)", p=OB)).then_inc(s_ix, 16)
            sp.wait_ge(s_ix, 48)

        @block.gpsimd
        def _(pool):
            nc.gpsimd.memset(fill[:], T).then_inc(s_f, 1)
            pool.wait_ge(s_ini, 16)
            pool.wait_ge(s_d, 1)
            for t in range(NT):
                R = rows(t)
                for j in range(TOPK):
                    nc.gpsimd.indirect_dma_start(out=table, out_offset=bass.IndirectOffsetOnAxis(ap=k.dest[:R, j, t:t + 1], axis=0),
                                                 in_=k.tok[:R, t:t + 1], in_offset=None).then_inc(s_sc, 16)

        @block.tensor
        def _(pe):
            pe.wait_ge(s_tb, 16)
            pe.wait_ge(s_b, 32)
            for m in range(6):
                mm = nc.tensor.transpose(bt[m // 4][:, m % 4, :], braw[:, m, :], C[:, at["ident"]])
            mm.then_inc(s_bt, 1)
            pe.wait_ge(s_m, 1)
            for t in range(NT):
                for u in range(t + 1):
                    nc.tensor.matmul(rk[:, t * NE:(t + 1) * NE], ones[:] if u < t else B[:, at["before"]], M[:, u, :],
                                     start=(u == 0), stop=(u == t))
            for u in range(NT):
                mm = nc.tensor.matmul(ct[:], ones[:], M[:, u, :], start=(u == 0), stop=(u == NT - 1))
            mm.then_inc(s_rk, 1)

        @block.scalar
        def _(act):
            act.wait_ge(s_e, 1)
            nc.scalar.activation(k.gates[:], k.gates[:], ACT.Exp).then_inc(s_ge, 1)

        @block.vector
        def _(dve):
            n_dc = [0]

            def link(ins):
                n_dc[0] += 1
                ins.then_inc(s_dc, 1)
                dve.wait_ge(s_dc, n_dc[0])

            V = nc.vector
            row = lambda ap: ap.unsqueeze(1).broadcast_to([P, NT, NE])
            L = k.logits
            V.memset(ones[:], 1.0)
            dve.wait_ge(s_tb, 16)
            link(V.tensor_scalar(e64[:], B[:, at["expert"]], -64.0, None, ALU.add))
            for j in range(TOPK):
                H = hot[:, j]
                link(V.tensor_reduce(tv[:, j, :], L[:], AX.X, ALU.max))
                link(V.tensor_tensor(t1[:], L[:], bc(tv[:, j, :], NE), ALU.is_equal))
                link(V.tensor_tensor(t1[:], t1[:], row(e64[:]), ALU.mult))
                link(V.tensor_reduce(ti[:], t1[:], AX.X, ALU.min))
                link(V.tensor_tensor(H, row(e64[:]), bc(ti[:], NE), ALU.is_equal))
                link(V.scalar_tensor_tensor(out=L[:].rearrange("p t e -> p (t e)"), in0=H.rearrange("p t e -> p (t e)"), scalar=NEG,
                                            in1=L[:].rearrange("p t e -> p (t e)"), op0=ALU.mult, op1=ALU.add))
            V.tensor_tensor(k.gates[:], tv[:], tv[:, 0:1, :].broadcast_to([P, TOPK, NT]), ALU.subtract).then_inc(s_e, 1)
            link(V.tensor_tensor(M[:], hot[:, 0], hot[:, 1], ALU.add))
            link(V.tensor_tensor(t1[:], hot[:, 2], hot[:, 3], ALU.add))
            link(V.tensor_tensor(M[:], M[:], t1[:], ALU.add))
            V.tensor_scalar(M[:, PT, :], M[:, PT, :], B[:, at["insample"]], None, ALU.mult).then_inc(s_m, 1)
            dve.wait_ge(s_ge, 1)
            link(V.tensor_reduce(gs[:], k.gates[:].rearrange("p j t -> p t j"), AX.X, ALU.add))
            link(V.reciprocal(gs[:], gs[:]))
            V.tensor_tensor(k.gates[:], k.gates[:], gs[:].unsqueeze(1).broadcast_to([P, TOPK, NT]), ALU.mult)
            dve.wait_ge(s_bt, 1)
            link(V.tensor_copy(k.buT[:], bt[0][:].rearrange("p a b -> p (a b)")))
            V.tensor_copy(k.bdT[:], bt[1][:, 0:2, :].rearrange("p a b -> p (a b)"))
            lin = k.buT[:].rearrange("p (e c) -> p e c", e=NE)[:, :, 8:16]
            V.tensor_scalar(lin, lin, 1.0, None, ALU.add)
            dve.wait_ge(s_rk, 1)
            V.memset(nb[:], 0.0)
            link(V.tensor_copy(cnt[:], ct[:]))
            for j in range(OB_MAX):
                link(V.scalar_tensor_tensor(out=nb[:], in0=cnt[:], scalar=float(CAP + j * OB), in1=nb[:], op0=ALU.is_gt, op1=ALU.add))
            link(V.tensor_tensor_scan(inc[:], ones[:, 0:NE], nb[:], 0.0, ALU.mult, ALU.add))
            link(V.tensor_tensor(st[:], inc[:], nb[:], ALU.subtract))
            link(V.tensor_scalar(st[:], st[:], float(OB), float(BASE - CAP), ALU.mult, ALU.add))
            r3 = rk[:].rearrange("p (t e) -> p t e", e=NE)
            link(V.tensor_tensor(alt[:], r3, row(st[:]), ALU.add))
            link(V.tensor_scalar(slot[:], r3, float(NE), None, ALU.mult))
            link(V.tensor_tensor(slot[:], slot[:], row(B[:, at["expert"]]), ALU.add))
            link(V.tensor_tensor(slot[:], slot[:], alt[:], ALU.subtract))
            link(V.tensor_scalar(t1[:], r3, float(CAP), None, ALU.is_lt))
            link(V.tensor_tensor(slot[:], slot[:], t1[:], ALU.mult))
            link(V.tensor_tensor(slot[:], slot[:], alt[:], ALU.add))
            for j in range(TOPK):
                link(V.tensor_tensor(t1[:], hot[:, j], slot[:], ALU.mult))
                link(V.tensor_reduce(df[:, j, :], t1[:], AX.X, ALU.add))
            V.tensor_copy(k.dest[:], df[:]).then_inc(s_d, 1)
            link(V.tensor_tensor(ob[:], inc[:].unsqueeze(1).broadcast_to([P, NOB, NE]), bc(B[:, at["blk"]], NE), ALU.is_le))
            link(V.tensor_reduce(obf[:], ob[:], AX.X, ALU.add))
            link(V.tensor_scalar(obf[:], obf[:], float(NE - 1), None, ALU.min))
            V.tensor_copy(k.obe[:, 0:NOB], obf[:])
            V.tensor_copy(k.obe[:, NOB:NOB + 1], inc[:, NE - 1:NE])
            link(V.memset(nb[:], 0.0))
            for w in WIDTHS[:-1]:
                link(V.scalar_tensor_tensor(out=nb[:], in0=cnt[:], scalar=float(w), in1=nb[:], op0=ALU.is_gt, op1=ALU.add))
            V.tensor_copy(k.wclass[:], nb[:])


def phase_experts(nc, k):
    i, at, C = k.i, k.at, k.C
    RB = CAP - P
    with ExitStack() as ctx:
        sb = lambda n, s, d=F32: ctx.enter_context(nc.sbuf_tensor(n, s, d))
        ps = lambda n, s, d=F32: ctx.enter_context(nc.psum_tensor(n, s, d))
        sem = k.sem
        W = k.W
        xg, xgB = sb("xg", [P, D]), sb("xgB", [RB, D])
        ix, ixB = sb("ix", [P, 1], I32), sb("ixB", [RB, 1], I32)
        hT, aT, yT = sb("hT", [P, KC, CAP]), sb("actT", [P, KC, CAP]), sb("yT", [P, KC, CAP])
        ysb = sb("y_rows", [P, 2, D])
        bu, bd = sb("b_up_cur", [P, 16]), sb("b_down_cur", [P, 8])
        gl, ln, sg, gm = (sb("glu", [P, 2, CAP]), sb("lin", [P, 2, CAP]), sb("sig", [P, 2, CAP]), sb("glusig", [P, 2, CAP]))
        up = [ps(f"up{j}", [P, 2, 256]) for j in range(2)]
        dn = [ps(f"down{j}", [P, 512]) for j in range(2)]
        xt = [ps(f"xt{j}", [P, 2, 256]) for j in range(2)]
        yt = [ps(f"yt{j}", [P, 4, P]) for j in range(2)]
        s_w = k.s_w
        s_ix, s_xg, s_xT, s_hT = sem("ix_copied"), sem("rows_gathered"), sem("rows_transposed"), sem("rowsT_ready")
        s_bu, s_up, s_gl, s_ln, s_sg, s_gm, s_a = (sem("b_up_ready"), sem("up_done"), sem("glu_ready"), sem("lin_ready"),
                                             sem("sigmoid_ready"), sem("glusig_ready"), sem("act_ready"))
        s_bd, s_dn, s_yT, s_yt, s_y, s_st = (sem("b_down_ready"), sem("down_done"), sem("yT_ready"), sem("y_transposed"),
                                             sem("y_rows_ready"), sem("y_stored"))
        s_carry = sem("wait_carrier")
        block = ctx.enter_context(nc.Block())
        ybase = k.y_dram[0:CAP * NE, :].rearrange("(r e) d -> r e d", e=NE)
        yover = k.y_dram[CAP * NE:NSLOT, :].rearrange("(b p) d -> p b d", p=OB)

        blk = lambda v, wide: v if wide else v + NE
        rows_in = lambda v, wide: v * 32 if wide else v * 16 + NE * 32
        ygroups = lambda v, wide: v * 4 if wide else v * 2 + NE * 4
        stores = lambda v, wide: v * 32 if wide else v * 16 + NE * 32

        def need(eng, semaphore, value, absorb=False):
            if isinstance(value, int) and value <= 0:
                return
            eng.wait_ge(semaphore, value)
            if absorb and not isinstance(value, int):
                eng.sem_inc(s_carry, 1)

        def overflow(eng, body):
            nblk = eng.value_load(k.obe[0:1, NOB:NOB + 1], min_val=0, max_val=NOB)
            with eng.If(nblk > 0):
                with eng.Fori(0, NOB) as b:
                    with eng.If(b < nblk):
                        body(b)

        def block_expert(eng, v, wide):
            return v if wide else eng.value_load(k.obe[0:1, bass.ds(v, 1)], min_val=0, max_val=NE - 1)

        @block.sync
        def _(sp):
            def body(v, wide):
                e, n = block_expert(sp, v, wide), blk(v, wide)
                for j in range(6):
                    need(sp, *((s_up, n * 8 + (2 * j + 2 - 8)) if j < 4 else (s_dn, n * 8 + (4 * (j - 4) + 4 - 8))))
                    load_piece(sp, k, e, j)

            with sp.Fori(1, NE) as e:
                body(e, True)
            overflow(sp, lambda b: body(b, False))

        @block.gpsimd
        def _(pool):
            def body(v, wide):
                n = blk(v, wide)
                need(pool, s_xT, n * 4)
                if wide:
                    nc.gpsimd.tensor_copy(ix[:], k.idxA[:, bass.ds(v, 1)])
                    nc.gpsimd.tensor_copy(ixB[:], k.idxB[:, bass.ds(v, 1)]).then_inc(s_ix, 1)
                else:
                    nc.gpsimd.tensor_copy(ix[:], k.idxO[:, bass.ds(v, 1)]).then_inc(s_ix, 1)
                need(pool, s_ix, n + 1, absorb=True)
                at_rows = lambda ap: bass.IndirectOffsetOnAxis(ap=ap, axis=0)
                nc.gpsimd.indirect_dma_start(out=xg[:], out_offset=None, in_=k.h_dram, in_offset=at_rows(ix[:, 0:1])).then_inc(s_xg, 16)
                if wide:
                    nc.gpsimd.indirect_dma_start(out=xgB[:], out_offset=None, in_=k.h_dram, in_offset=at_rows(ixB[:, 0:1])).then_inc(s_xg, 16)

            body(0, True)
            with pool.Fori(1, NE) as e:
                body(e, True)
            overflow(pool, lambda b: body(b, False))

        @block.tensor
        def _(pe):
            ident = C[:, at["ident"]]

            def turn_x(v, wide, groups=range(4)):
                n = blk(v, wide)
                if 0 in groups:
                    need(pe, s_xg, rows_in(v, wide) + (32 if wide else 16))
                for j in groups:
                    need(pe, s_hT, n * 4 + max(j - 1, 0))
                    for m in range(2):
                        c = slice((2 * j + m) * P, (2 * j + m + 1) * P)
                        mm = nc.tensor.transpose(xt[j % 2][:, m, 0:P], xg[:, c], ident)
                        if wide:
                            mm = nc.tensor.transpose(xt[j % 2][:, m, P:CAP], xgB[:, c], ident[:RB, :RB])
                    mm.then_inc(s_xT, 1)

            def by_width(v, ahead):
                c = pe.value_load(k.wclass[0:1, bass.ds(v, 1)], min_val=0, max_val=len(WIDTHS) - 1)
                for j, N in enumerate(WIDTHS):
                    with pe.If(c == j):
                        body(v, True, ahead, N)

            def turn_y(v, wide, j):
                r0, r1 = (0, P) if j < 2 else (P, CAP)
                need(pe, s_yT, blk(v, wide) * 8 + 4 * (j % 2) + 4)
                need(pe, s_y, ygroups(v, wide) + max(j - 1, 0), absorb=True)
                for m in range(4):
                    mm = nc.tensor.transpose(yt[j % 2][:r1 - r0, m, :], yT[:, 4 * (j % 2) + m, r0:r1], ident)
                mm.then_inc(s_yt, 1)

            def body(v, wide, ahead, N=OB, behind=True):
                n = blk(v, wide)
                if not wide:
                    turn_x(v, False)
                need(pe, s_hT, n * 4 + 4)
                for c in range(8):
                    if c % 2 == 0:
                        need(pe, s_w[c // 2], n * 32 + 32)
                    need(pe, s_ln, n * 8 + max(c - 1, 0))
                    for h in range(2):
                        w0 = h * 256 + (c % 2) * P
                        for kk in range(KC):
                            mm = nc.tensor.matmul(up[c % 2][:, h, :N], W[c // 2][:, kk, w0:w0 + P], hT[:, kk, :N],
                                                  start=(kk == 0), stop=(kk == KC - 1))
                    mm.then_inc(s_up, 1)
                    if wide and behind and 1 <= c <= 4:
                        turn_y(v - 1, True, c - 1)
                if ahead:
                    turn_x(v + 1, wide, (0, 1))
                for d in range(8):
                    if d % 4 == 0:
                        need(pe, s_w[4 + d // 4], n * 16 + 16)
                    need(pe, s_yT, n * 8 + max(d - 1, 0))
                    for kk in range(KC):
                        if d == 0:
                            need(pe, s_a, n * 8 + kk + 1)
                        mm = nc.tensor.matmul(dn[d % 2][:, :N], W[4 + d // 4][:, kk, (d % 4) * P:(d % 4) * P + P], aT[:, kk, :N],
                                              start=(kk == 0), stop=(kk == KC - 1))
                    mm.then_inc(s_dn, 1)
                    if ahead and d < 2:
                        turn_x(v + 1, wide, (2 + d,))
                if not wide:
                    for j in range(2):
                        turn_y(v, False, j)

            turn_x(0, True)
            body(0, True, True, CAP, behind=False)
            with pe.Fori(1, NE - 1) as e:
                by_width(e, True)
            by_width(NE - 1, False)
            for j in range(4):
                turn_y(NE - 1, True, j)
            overflow(pe, lambda b: body(b, False, False))

        @block.scalar
        def _(act):
            def rows_out(v, wide, j):
                R = P if j < 2 else RB
                if j == 0:
                    need(act, s_st, stores(v, wide))
                need(act, s_yt, ygroups(v, wide) + j + 1)
                nc.scalar.copy(ysb[:R, j // 2, (j % 2) * 512:(j % 2) * 512 + 512],
                               yt[j % 2][:R].rearrange("p a b -> p (a b)")).then_inc(s_y, 1)
                if j % 2 == 1:
                    need(act, s_y, ygroups(v, wide) + j + 1)
                    dst = (ybase[0:P] if j == 1 else ybase[P:CAP])[:, bass.ds(v, 1), :] if wide else yover[:, bass.ds(v, 1), :]
                    act.dma_start(dst.rearrange("p o d -> p (o d)"), ysb[:R, j // 2, :]).then_inc(s_st, 16)

            def body(v, wide, behind=True):
                N, e, n = CAP if wide else OB, block_expert(act, v, wide), blk(v, wide)
                need(act, s_yT, n * 8)
                nc.scalar.copy(bd[:], k.bdT[:, bass.ds(e * 8, 8)]).then_inc(s_bd, 1)
                for c in range(8):
                    need(act, s_gl, n * 8 + c + 1)
                    nc.scalar.activation(sg[:, c % 2, :N], gl[:, c % 2, :N], ACT.Sigmoid, scale=ALPHA).then_inc(s_sg, 1)
                    if wide and behind and 1 <= c <= 4:
                        rows_out(v - 1, True, c - 1)
                need(act, s_bd, n + 1)
                for d in range(8):
                    need(act, s_dn, n * 8 + d + 1)
                    nc.scalar.activation(yT[:, d, :N], dn[d % 2][:, :N], ACT.Identity, bias=bd[:, d:d + 1]).then_inc(s_yT, 1)
                if not wide:
                    for j in range(2):
                        rows_out(v, False, j)

            body(0, True, behind=False)
            with act.Fori(1, NE) as e:
                body(e, True)
            for j in range(4):
                rows_out(NE - 1, True, j)
            overflow(act, lambda b: body(b, False))
            nblk = act.value_load(k.obe[0:1, NOB:NOB + 1], min_val=0, max_val=NOB)
            need(act, s_st, nblk * 16 + NE * 32, absorb=True)

        @block.vector
        def _(dve):
            def take_x(v, wide):
                n, N = blk(v, wide), CAP if wide else OB
                for j in range(4):
                    need(dve, s_xT, n * 4 + j + 1)
                    nc.vector.tensor_copy(hT[:, 2 * j:2 * j + 2, :N], xt[j % 2][:, :, :N]).then_inc(s_hT, 1)

            def body(v, wide, ahead):
                N, e, n = CAP if wide else OB, block_expert(dve, v, wide), blk(v, wide)
                if not wide:
                    take_x(v, False)
                nc.vector.tensor_copy(bu[:], k.buT[:, bass.ds(e * 16, 16)]).then_inc(s_bu, 1)
                need(dve, s_bu, n + 1)
                for c in range(8):
                    b = c % 2
                    need(dve, s_up, n * 8 + c + 1)
                    nc.vector.tensor_scalar(gl[:, b, :N], up[b][:, 0, :N], bu[:, c:c + 1], LIMIT, ALU.add, ALU.min).then_inc(s_gl, 1)
                    nc.vector.tensor_scalar(ln[:, b, :N], up[b][:, 1, :N], bu[:, 8 + c:9 + c], 1.0 - LIMIT, ALU.add, ALU.max).then_inc(s_ln, 1)
                    need(dve, s_sg, n * 8 + c + 1)
                    nc.vector.tensor_tensor(gm[:, b, :N], gl[:, b, :N], sg[:, b, :N], ALU.mult).then_inc(s_gm, 1)
                    need(dve, s_gm, n * 8 + c + 1)
                    nc.vector.scalar_tensor_tensor(out=aT[:, c, :N], in0=ln[:, b, :N], scalar=1.0 + LIMIT, in1=gm[:, b, :N],
                                                   op0=ALU.min, op1=ALU.mult).then_inc(s_a, 1)
                if ahead:
                    take_x(v + 1, wide)

            take_x(0, True)
            body(0, True, True)
            with dve.Fori(1, NE - 1) as e:
                body(e, True, True)
            body(NE - 1, True, False)
            overflow(dve, lambda b: body(b, False, False))


def phase_combine(nc, k):
    with ExitStack() as ctx:
        sb = lambda n, s, d=F32: ctx.enter_context(nc.sbuf_tensor(n, s, d))
        sem = k.sem
        NB = 3
        x = [sb(f"x2h{j}", [P, D]) for j in range(NB)]
        y = [[sb(f"yk{j}{m}", [P, D]) for m in range(TOPK)] for j in range(NB)]
        s_x, s_y, s_st = ([sem(f"h_{n}{j}") for j in range(NB)] for n in ("x2_loaded", "y_gathered", "stored"))
        s_a, s_dc = sem("combined"), sem("combine_dve_chain")
        block = ctx.enter_context(nc.Block())

        @block.sync
        def _(sp):
            def load(t):
                if t >= NB:
                    sp.wait_ge(s_st[t % NB], 16 * (t // NB))
                sp.dma_start(x[t % NB][:rows(t), :], k.x2_dram[t * P:t * P + rows(t), :]).then_inc(s_x[t % NB], 16)

            for t in range(NB):
                load(t)
            for t in range(NT):
                sp.wait_ge(s_a, t + 1)
                dst = k.o["xp"][0, t * P:t * P + P, :] if t < PT else k.o["xs"].rearrange("b s d -> (b s) d")
                sp.dma_start(dst, x[t % NB][:rows(t), :]).then_inc(s_st[t % NB], 16)
                if t + NB < NT:
                    load(t + NB)
            for j in range(NB):
                sp.wait_ge(s_st[j], 16 * len(range(j, NT, NB)))

        @block.gpsimd
        def _(pool):
            for t in range(NT):
                if t >= NB:
                    pool.wait_ge(s_a, t - NB + 1)
                for m in range(TOPK):
                    nc.gpsimd.indirect_dma_start(out=y[t % NB][m][:rows(t), :], out_offset=None, in_=k.y_dram,
                                                 in_offset=bass.IndirectOffsetOnAxis(ap=k.dest[:rows(t), m, t:t + 1], axis=0)).then_inc(s_y[t % NB], 16)

        @block.vector
        def _(dve):
            n_dc = 0
            for t in range(NT):
                R, xx = rows(t), x[t % NB]
                dve.wait_ge(s_x[t % NB], 16 * (t // NB + 1))
                dve.wait_ge(s_y[t % NB], 16 * TOPK * (t // NB + 1))
                for m in range(TOPK):
                    ins = nc.vector.scalar_tensor_tensor(out=xx[:R, :], in0=y[t % NB][m][:R, :], scalar=k.gates[:R, m, t:t + 1],
                                                         in1=xx[:R, :], op0=ALU.mult, op1=ALU.add)
                    if m < TOPK - 1:
                        ins.then_inc(s_dc, 1)
                        n_dc += 1
                        dve.wait_ge(s_dc, n_dc)
                ins.then_inc(s_a, 1)



def program(nc, i, o, at):
    k = Ctx()
    k.i, k.o = i, o
    with ExitStack() as ctx:
        taken = []

        def sem(name):
            taken.append(nc.alloc_semaphore(name))
            return taken[-1]

        def recycle():
            nc.clear_and_free_semaphores(taken)
            nc.all_engine_barrier()
            taken.clear()

        k.sem = sem
        k.at = {n: slice(a, a + w) for n, (a, w) in at.items()}
        dram = lambda n, s, d=F32: nc.dram_tensor(n, s, d, kind="Internal").ap()
        k.h_dram, k.x2_dram, k.y_dram = dram("h_rows", (T + 1, D)), dram("x2_rows", (T, D)), dram("y_slots", (NSLOT, D))
        k.slot_dram = dram("slot_tokens", (NSLOT, 1), I32)
        sb = lambda n, s, d=F32: ctx.enter_context(nc.sbuf_tensor(n, s, d))
        k.C = sb("tables_sb", [P, i["tables_a"].shape[1]])
        k.tok = sb("tokens_sb", [P, NT], I32)
        k.logits = sb("logits", [P, NT, NE])
        with ExitStack() as att:
            sb = lambda n, s, d=F32: att.enter_context(nc.sbuf_tensor(n, s, d))
            k.qT = sb("qT", [P, 4, T])
            k.ksT = sb("ksT", [P, T])
            k.kwT = sb("kwT", [P, T])
            k.mqT = sb("mqT", [P, 2, T])
            k.mkT = sb("mkT", [P, 2, NMEM])
            k.mv = sb("mv", [P, MT, 256])
            k.vs = sb("vs", [P, NT, P])
            k.vw = sb("vw", [P, NT, P])
            k.gate = sb("gate", [P, NT, 24])
            k.rg = sb("rg", [P, NT, 256])
            k.oret = sb("oret", [P, NT, 256])
            k.rT = sb("rT", [P, 6, P])
            k.rot = sb("rot", [P, 512])
            k.kz = sb("kz", [P, 256])
            k.rvs = sb("rvs", [SR, 256])
            k.pages = sb("pages", [1, DB * PAGES], I32)
            k.Rst = sb("Rst", [P, 2, HD])
            phase_project(nc, k)
            k.B = sb("tables_b_sb", [P, i["tables_b"].shape[1]])
            k.kcT = sb("kcT", [P, DB + 1, NCMP])
            k.vc = sb("vc", [NCMP, DB + 1, P])
            phase_compress(nc, k)
            k.mixT = sb("mixT", [P, KC, T])
            recycle()
            phase_prompt(nc, k)
            with ExitStack() as dec:
                k.nat = dec.enter_context(nc.sbuf_tensor("cache_rows", [P, DB // 2, PAGES, 256], F32))
                k.natw = dec.enter_context(nc.sbuf_tensor("window_rows", [P, DB // 2, 4, 256], F32))
                k.s_cache = [sem(f"caches_loaded{j}") for j in range(3)]
                k.s_cache_pool = [sem(f"pool_caches_loaded{j}") for j in range(2)]
                k.w_out = k.nat[:].rearrange("p b s x -> p (b s x)").rearrange("p (c n) -> p c n", c=KC)
                k.s_w_out = [sem(f"w_out_loaded{j}") for j in range(2)]
                phase_retention_out(nc, k)
                phase_sample(nc, k)
                phase_out(nc, k)
        recycle()
        sb = lambda n, s, d=F32: ctx.enter_context(nc.sbuf_tensor(n, s, d))
        k.gates = sb("gates", [P, TOPK, NT])
        k.dest = sb("dest", [P, TOPK, NT], I32)
        k.obe = sb("overflow_experts", [P, NOB + 1], I32)
        k.wclass = sb("width_class", [P, NE], I32)
        k.buT, k.bdT = sb("b_up_T", [P, NE * 16]), sb("b_down_T", [P, NE * 8])
        k.idxA, k.idxB = sb("idx_first", [P, NE], I32), sb("idx_second", [CAP - P, NE], I32)
        k.idxO = sb("idx_overflow", [OB, NOB], I32)
        k.W = [sb(f"w_piece{j}", [P, KC, 512]) for j in range(6)]
        k.s_w = [sem(f"piece_loaded{j}") for j in range(6)]
        with ExitStack() as route:
            k.B = route.enter_context(nc.sbuf_tensor("tables_b_again", [P, i["tables_b"].shape[1]], F32))
            phase_route(nc, k)
        phase_experts(nc, k)
        phase_combine(nc, k)


_INS = ['x_prompt', 'x_sample', 'mem_prompt', 'cache_cmp_kv', 'cache_slc_kv', 'cache_win_kv', 'state_ret',
        'cache_mem_kv', 'page_table', 'norm1_g', 'w_in', 'q_norm_g', 'k_norm_cmp_g', 'k_norm_slc_g', 'k_norm_win_g',
        'cmp_pe_k', 'cmp_w1_k', 'cmp_w2_k', 'cmp_pe_v', 'cmp_w1_v', 'cmp_w2_v', 'ret_norm_g', 'mem_norm_g',
        'w_mem_kv', 'mem_q_norm_g', 'mem_k_norm_g', 'w_out', 'norm2_g', 'w_router', 'b_router', 'w_up', 'b_up',
        'w_down', 'b_down']
_OUTS = [("xp", (1, S, D)), ("xs", (DB, QS, D)), ("cmp_p", (1, 1, S, 2, G, HD)), ("slc_p", (1, 1, S, 2, G, HD)),
         ("win_p", (1, 1, WIN, 2, G, HD)), ("ret_p", (1, 1, 4, HD, HD)), ("mem_p", (1, 1, NMEM, 2, 4, HD)),
         ("cmp_s", (1, DB, QS, 2, G, HD)), ("slc_s", (1, DB, QS, 2, G, HD)), ("win_s", (1, DB, WIN, 2, G, HD)),
         ("ret_s", (1, DB, 4, HD, HD))]


def kernel(**inputs):
    import numpy as _np
    import concourse.bacc as _bacc
    from concourse import mybir as _mybir
    from concourse.bass_utils import run_bass_kernel_spmd as _run

    nc = _bacc.Bacc("TRN2", target_bir_lowering=False, num_devices=1)
    (tables_a, tables_b), at, tokens = shape_tables()
    arrays, i, o = {}, {}, {}
    given = {n: _np.ascontiguousarray(inputs[n]) for n in _INS}
    given["tables_a"], given["tables_b"] = tables_a, tables_b
    given["tokens"] = tokens
    for n, a in given.items():
        arrays[f"in_{n}"] = a
        i[n] = nc.dram_tensor(f"in_{n}", a.shape, _mybir.dt.from_np(a.dtype), kind="ExternalInput").ap()
    for n, shape in _OUTS:
        o[n] = nc.dram_tensor(f"out_{n}", shape, _mybir.dt.float32, kind="ExternalOutput").ap()
    program(nc, i, o, at)
    r = _run(nc, [arrays], core_ids=[0])
    return tuple(r.results[0][f"out_{n}"] for n, _ in _OUTS)
```
